# Optimizing a Trainium2 kernel written in Bass

```python
import functools
import jax, jax.numpy as jnp
from jax import lax
import numpy as np

D_MODEL = 1024
BATCH = 1
SEQ = 512
DEPTH = 2
DEC_BATCH = 8
DEC_SEQ = 1
PAST_LEN = 256
PAGE_SIZE = 128

N_PAGES = PAST_LEN // PAGE_SIZE
HEAD_DIM = 64
W_A = D_MODEL // 2
W_B = D_MODEL - W_A
H_A = W_A // HEAD_DIM
H_B = W_B // HEAD_DIM
H_IDX = 4
D_IDX = 64
TOPK_MAX = 256
D_FF = 4 * D_MODEL
ROPE_THETA = 10000.0
EPS = 1e-6
Q_BLOCK = 128
RET_CHUNK = 128
COL_SIZES = (W_A, W_A, W_A, H_IDX * D_IDX, D_IDX, H_IDX, W_B, W_B, W_B, W_B)
N_IN = sum(COL_SIZES)

kernel_name = "hymba_dsa_retention_decoder_step"

F32 = jnp.float32

def rmsnorm(x, g):
    xf = x.astype(F32)
    y = xf * lax.rsqrt(jnp.mean(xf * xf, axis=-1, keepdims=True) + EPS)
    return (y * g.astype(F32)).astype(x.dtype)

def rope(x, pos):
    half = x.shape[-1] // 2
    inv = ROPE_THETA ** (-jnp.arange(half, dtype=F32) / half)
    ang = pos[:, None] * inv[None, :]
    c = jnp.cos(ang)[None, :, None, :]
    s = jnp.sin(ang)[None, :, None, :]
    xf = x.astype(F32)
    x1, x2 = xf[..., :half], xf[..., half:]
    return jnp.concatenate([x1 * c - x2 * s, x1 * s + x2 * c], axis=-1).astype(x.dtype)

def project_mixers(h, w_in_l, pos):
    B, T, _ = h.shape
    z = h @ w_in_l
    splits = np.cumsum(COL_SIZES)[:-1].tolist()
    qa, ka, va, qi, ki, wi, qb, kb, vb, gb = jnp.split(z, splits, axis=-1)
    qa = rope(qa.reshape(B, T, H_A, HEAD_DIM), pos)
    ka = rope(ka.reshape(B, T, H_A, HEAD_DIM), pos)
    va = va.reshape(B, T, H_A, HEAD_DIM)
    qi = rope(qi.reshape(B, T, H_IDX, D_IDX), pos)
    ki = rope(ki.reshape(B, T, 1, D_IDX), pos)[:, :, 0]
    wi = wi * (H_IDX ** -0.5 * D_IDX ** -0.5)
    qb = rope(qb.reshape(B, T, H_B, HEAD_DIM), pos)
    kb = rope(kb.reshape(B, T, H_B, HEAD_DIM), pos) * (HEAD_DIM ** -0.5)
    vb = vb.reshape(B, T, H_B, HEAD_DIM)
    return qa, ka, va, qi, ki, wi, qb, kb, vb, gb

def indexer_scores(qi, ki, wi):
    dots = jnp.einsum('bthd,bsd->bths', qi.astype(F32), ki.astype(F32))
    return jnp.einsum('bth,bths->bts', wi.astype(F32), jax.nn.relu(dots))

def sparse_attend(q, kg, vg, valid):
    s = jnp.einsum('bthd,btkhd->bthk', q.astype(F32), kg.astype(F32)) * (HEAD_DIM ** -0.5)
    s = jnp.where(valid[:, :, None, :], s, -jnp.inf)
    p = jax.nn.softmax(s, axis=-1)
    return jnp.einsum('bthk,btkhd->bthd', p, vg.astype(F32)).astype(q.dtype)

def gather_rows(src, idx):
    return jax.vmap(lambda s_, i_: s_[i_])(src, idx)

def dsa_prompt(qa, ka, va, qi, ki, wi):
    B, T = qa.shape[:2]
    topk = min(TOPK_MAX, T // 4)
    nb = T // Q_BLOCK
    key_pos = jnp.arange(T)

    def blocks(a):
        return a.reshape((B, nb, Q_BLOCK) + a.shape[2:]).swapaxes(0, 1)

    def one_block(args):
        q_blk, qi_blk, wi_blk, t0 = args
        tq = t0 + jnp.arange(Q_BLOCK)
        sc = indexer_scores(qi_blk, ki, wi_blk)
        sc = jnp.where((key_pos[None, :] <= tq[:, None])[None], sc, -jnp.inf)
        _, sel = lax.top_k(sc, topk)
        valid = sel <= tq[None, :, None]
        return sparse_attend(q_blk, gather_rows(ka, sel), gather_rows(va, sel), valid)

    out = lax.map(one_block, (blocks(qa), blocks(qi), blocks(wi), jnp.arange(nb) * Q_BLOCK))
    return out.swapaxes(0, 1).reshape(B, T, H_A, HEAD_DIM)

def dsa_sample(qa, ka, va, qi, ki, wi, pool_k, pool_v, pool_ki, page_table):
    B, T = qa.shape[:2]
    past = page_table.shape[1] * PAGE_SIZE
    L = past + T
    topk = min(TOPK_MAX, L // 4)
    phys = (page_table[:, :, None] * PAGE_SIZE + jnp.arange(PAGE_SIZE)[None, None, :]).reshape(B, past)
    flat_k = pool_k.reshape(-1, H_A, HEAD_DIM)
    flat_v = pool_v.reshape(-1, H_A, HEAD_DIM)
    flat_ki = pool_ki.reshape(-1, D_IDX)
    ki_all = jnp.concatenate([flat_ki[phys], ki], axis=1)
    tq = past + jnp.arange(T)
    sc = indexer_scores(qi, ki_all, wi)
    sc = jnp.where((jnp.arange(L)[None, :] <= tq[:, None])[None], sc, -jnp.inf)
    _, sel = lax.top_k(sc, topk)
    valid = sel <= tq[None, :, None]
    in_past = (sel < past)[..., None, None]
    rows = jnp.take_along_axis(phys, jnp.clip(sel, 0, past - 1).reshape(B, -1), axis=1).reshape(sel.shape)
    new_idx = jnp.clip(sel - past, 0, T - 1)
    kg = jnp.where(in_past, flat_k[rows], gather_rows(ka, new_idx))
    vg = jnp.where(in_past, flat_v[rows], gather_rows(va, new_idx))
    return sparse_attend(qa, kg, vg, valid)

def retention(q, k, v, s0):
    B, L, H, D = q.shape
    C = RET_CHUNK if L % RET_CHUNK == 0 else L
    n = L // C
    lg = jnp.log1p(-jnp.exp2(-5.0 - jnp.arange(H, dtype=F32)))
    i = jnp.arange(C, dtype=F32)
    diff = i[:, None] - i[None, :]
    dmask = jnp.where(diff[None] >= 0, jnp.exp(jnp.maximum(diff, 0.0)[None] * lg[:, None, None]), 0.0)
    q_dec = jnp.exp((i[:, None] + 1.0) * lg[None, :])
    k_dec = jnp.exp((C - 1.0 - i)[:, None] * lg[None, :])
    c_dec = jnp.exp(C * lg)

    def chunks(a):
        return a.astype(F32).reshape(B, n, C, H, D).swapaxes(0, 1)

    def step(S, qkv):
        qc, kc, vc = qkv
        att = jnp.einsum('bihd,bjhd->bhij', qc, kc) * dmask[None]
        o = (jnp.einsum('bhij,bjhe->bihe', att, vc)
             + jnp.einsum('bihd,bhde->bihe', qc, S) * q_dec[None, :, :, None])
        S = S * c_dec[None, :, None, None] + jnp.einsum('bjhd,bjhe->bhde', kc * k_dec[None, :, :, None], vc)
        return S, o

    S, o = lax.scan(step, s0.astype(F32), (chunks(q), chunks(k), chunks(v)))
    return o.swapaxes(0, 1).reshape(B, L, H, D), S

def retention_mixer(qb, kb, vb, gb, s0, g_ret_l):
    o, S = retention(qb, kb, vb, s0)
    mu = jnp.mean(o, axis=-1, keepdims=True)
    var = jnp.mean(jnp.square(o - mu), axis=-1, keepdims=True)
    o = (o - mu) * lax.rsqrt(var + EPS)
    B, T = o.shape[:2]
    o = o.reshape(B, T, W_B) * g_ret_l.astype(F32)
    return (o * jax.nn.silu(gb.astype(F32))).astype(gb.dtype), S

def trunk_layer(x, l, pos, mixer_a, s0, w_in, w_out, g_ret, g_mix_pre, g_mix_post,
                g_ffn_pre, g_ffn_post, w_up, w_down):
    B, T = x.shape[:2]
    h = rmsnorm(x, g_mix_pre[l])
    qa, ka, va, qi, ki, wi, qb, kb, vb, gb = project_mixers(h, w_in[l], pos)
    a = mixer_a(qa, ka, va, qi, ki, wi)
    b, S = retention_mixer(qb, kb, vb, gb, s0, g_ret[l])
    m = jnp.concatenate([a.reshape(B, T, W_A), b], axis=-1) @ w_out[l]
    x = x + rmsnorm(m, g_mix_post[l])
    f = jnp.square(jax.nn.relu(rmsnorm(x, g_ffn_pre[l]) @ w_up[l])) @ w_down[l]
    x = x + rmsnorm(f, g_ffn_post[l])
    return x, ka, va, ki, S.astype(s0.dtype)

def setup_inputs(seed: int = 0) -> dict:
    key = jax.random.key(seed)
    ks = jax.random.split(key, 20)
    used = DEC_BATCH * N_PAGES
    n_pool = used + max(1, used // 4)
    nrm = jax.random.normal

    def gain(k, shape):
        return 1.0 + 0.05 * nrm(k, shape, F32)

    page_table = jax.random.permutation(ks[0], n_pool)[:used].reshape(DEC_BATCH, N_PAGES).astype(jnp.int32)
    return {
        "x_prompt": nrm(ks[1], (BATCH, SEQ, D_MODEL), F32),
        "x_sample": nrm(ks[2], (DEC_BATCH, DEC_SEQ, D_MODEL), F32),
        "cache_k": nrm(ks[3], (DEPTH, n_pool, PAGE_SIZE, H_A, HEAD_DIM), F32),
        "cache_v": nrm(ks[4], (DEPTH, n_pool, PAGE_SIZE, H_A, HEAD_DIM), F32),
        "cache_kidx": nrm(ks[5], (DEPTH, n_pool, PAGE_SIZE, D_IDX), F32),
        "state_ret": nrm(ks[6], (DEPTH, DEC_BATCH, H_B, HEAD_DIM, HEAD_DIM), F32),
        "page_table": page_table,
        "w_in": nrm(ks[7], (DEPTH, D_MODEL, N_IN), F32) * D_MODEL ** -0.5,
        "w_out": nrm(ks[8], (DEPTH, D_MODEL, D_MODEL), F32) * D_MODEL ** -0.5,
        "g_ret": gain(ks[9], (DEPTH, W_B)),
        "g_mix_pre": gain(ks[10], (DEPTH, D_MODEL)),
        "g_mix_post": gain(ks[11], (DEPTH, D_MODEL)),
        "g_ffn_pre": gain(ks[12], (DEPTH, D_MODEL)),
        "g_ffn_post": gain(ks[13], (DEPTH, D_MODEL)),
        "w_up": nrm(ks[14], (DEPTH, D_MODEL, D_FF), F32) * D_MODEL ** -0.5,
        "w_down": nrm(ks[15], (DEPTH, D_FF, D_MODEL), F32) * D_FF ** -0.5,
    }

def reference(x_prompt, x_sample, cache_k, cache_v, cache_kidx, state_ret, page_table,
              w_in, w_out, g_ret, g_mix_pre, g_mix_post, g_ffn_pre, g_ffn_post, w_up, w_down):
    weights = (w_in, w_out, g_ret, g_mix_pre, g_mix_post, g_ffn_pre, g_ffn_post, w_up, w_down)
    past = page_table.shape[1] * PAGE_SIZE
    pos_p = jnp.arange(x_prompt.shape[1], dtype=F32)
    pos_s = past + jnp.arange(x_sample.shape[1], dtype=F32)
    s0_p = jnp.zeros((x_prompt.shape[0], H_B, HEAD_DIM, HEAD_DIM), x_prompt.dtype)
    yp, ys = x_prompt, x_sample
    kp, vp, kip, sp, kss, vss, kis, ss = [], [], [], [], [], [], [], []
    for l in range(DEPTH):
        yp, k_, v_, ki_, S_ = trunk_layer(yp, l, pos_p, dsa_prompt, s0_p, *weights)
        kp.append(k_); vp.append(v_); kip.append(ki_); sp.append(S_)
        mix_s = functools.partial(dsa_sample, pool_k=cache_k[l], pool_v=cache_v[l],
                                  pool_ki=cache_kidx[l], page_table=page_table)
        ys, k_, v_, ki_, S_ = trunk_layer(ys, l, pos_s, mix_s, state_ret[l], *weights)
        kss.append(k_); vss.append(v_); kis.append(ki_); ss.append(S_)
    return (yp, ys, jnp.stack(kp), jnp.stack(vp), jnp.stack(kip), jnp.stack(sp),
            jnp.stack(kss), jnp.stack(vss), jnp.stack(kis), jnp.stack(ss))


_drawn_inputs = setup_inputs


def setup_inputs(seed=0):
    import zlib

    import numpy as np

    out = dict(_drawn_inputs(seed))
    spreads = {}
    factors = {}
    for name, (base, spread) in spreads.items():
        noise = np.random.default_rng([zlib.crc32(name.encode()), seed]).standard_normal(out[name].shape)
        drawn = base * np.exp(spread * noise) if base else spread * noise
        out[name] = __import__('jax').numpy.asarray(drawn.astype(out[name].dtype))
    for name, factor in factors.items():
        out[name] = (out[name] * factor).astype(out[name].dtype)
    return out
```

```python
import numpy as np
import concourse.bass as bass
from concourse import mybir
from contextlib import ExitStack

F32 = mybir.dt.float32
I32 = mybir.dt.int32
ALU = mybir.AluOpType
ACT = mybir.ActivationFunctionType
AX_X = mybir.AxisListType.X

D = 1024
DEPTH = 2
SEQ = 512
NB = 8
PAGE = 128
NPAGES = 2
PAST = PAGE * NPAGES
L = PAST + 1
HD = 64
NH = 8
NI = 4
FF = 4 * D
P = 128
KD = D // P
TOK = SEQ + NB
HALF = TOK // 2
NT = SEQ // P
TILES = NT + 1
TOPK_P = min(256, SEQ // 4)
TOPK_S = min(256, L // 4)
W = 512
W_IDX = NI * HD + HD + NI
UNIT = 2048
SLOTS = 4
U_PROJ, U_OUT, U_UP = 16, 4, 8
UNITS = U_PROJ + U_OUT + 4 * U_UP
FT = 16
CSLOTS = 3
EPS = 1e-6
NEG = -1e30
MARK = -3e38
ATT_SCALE = HD ** -0.5


def rows(t):
    return P if t < NT else NB


def token_cols(t):
    return slice(t * P, t * P + rows(t))


def counter():
    n = {}

    def up(sem):
        n[sem.num] = n.get(sem.num, 0) + 1
        return n[sem.num]

    return n, up


def build(nc, x, w_idx, w_all, gains, g_ret, cache_k, cache_v, cache_ki, state, pages, tab_cos, tab_sin,
          dmask, k_decay, q_decay, c_decay, s_gamma, ident, expand, select, diag, causal,
          y, k_out, v_out, ki_out, ret_out, ks_out, vs_out, kis_out, rets_out):
    ctx = ExitStack()
    with ctx:
        def sb(name, shape, dt=F32):
            return ctx.enter_context(nc.sbuf_tensor(name, shape, dt))

        x_feat = sb("x_feat", [P, KD, TOK])
        h_feat = sb("h_feat", [P, KD, TOK])
        mix = sb("mix", [P, KD, TOK])
        wring = [sb(f"wring{i}", [P, UNIT]) for i in range(SLOTS)]
        big = sb("big", [P, 4 * TILES * W + 3 * 4 * SEQ])
        ff = big[:, 0:FT * TOK].rearrange("p (j n) -> p j n", n=TOK)
        osb = big[:, FT * TOK:(FT + KD) * TOK].rearrange("p (j n) -> p j n", n=TOK)
        at = [0]

        def part(size, **kw):
            at[0] += size
            return big[:, at[0] - size:at[0]].rearrange("p (t n) -> p t n", **kw)

        zr = [part(TILES * W, n=W) for _ in range(2)]
        v_tok = part(TILES * W, n=W)
        gate = part(TILES * W, n=W)
        qT = part(4 * SEQ, n=SEQ)
        kT = part(4 * SEQ, n=SEQ)
        kbd = part(NT * W, n=W)
        qz = [sb(f"qz{i}", [P, NH, P]) for i in range(2)]
        qiT = kbd[:, 0:2, :]
        kiz = [qz[0][:, j:NH:2, :] for j in range(2)]
        wi = sb("wi", [P, TILES, NI])
        bias = sb("bias", [P, 128 + 256 + 384 + 512])
        b_at = [0, 128, 384, 768]
        top8 = sb("top8", [P, 8])
        s_sbw = [sb(f"s_sb{i}", [P, TOK]) for i in range(2)]
        s_sb = [a[:, 0:W] for a in s_sbw]
        p_sbw = [sb(f"p_sb{i}", [P, TOK]) for i in range(2)]
        p_sb = [a[:, 0:W] for a in p_sbw]
        pt_sbw = [sb(f"pt_sb{i}", [P, TOK]) for i in range(2)]
        pt_sb = [a[:, 0:W] for a in pt_sbw]
        temps = sb("temps", [P, 3 * TOK])
        sqr = [temps[:, i * TOK:(i + 1) * TOK] for i in range(3)]
        attm = temps[:, 0:NH * P].rearrange("p (h n) -> p h n", n=P)
        qTd = temps[:, NH * P:NH * P + 4 * P].rearrange("p (h n) -> p h n", n=P)
        raw = [pt_sb[0], pt_sb[1], temps[:, 0:W]]
        rt = p_sb
        s_bd = sb("s_bd", [P, 4, P])
        s_tmp = s_sb[0][:, 0:4 * HD].rearrange("p (h d) -> p h d", d=HD)
        mx = sb("mx", [P, 2]); neg_mx = sb("neg_mx", [P, 2])
        rsum = sb("rsum", [P, 2]); rinv = sb("rinv", [P, 2])
        gn_mu = sb("gn_mu", [P, TILES, NH]); gn_var = sb("gn_var", [P, TILES, NH])
        ssum, std, upd = pt_sbw[0], s_sbw[0], s_sbw[1]
        rstd = [sb("rstd0", [P, TOK]), p_sbw[0]]
        rtok = sb("rtok", [P, 3, TILES])
        gate_flat = gate.rearrange("p t n -> p (t n)")
        kit = gate_flat[0:HD, 0:NB * L].rearrange("p (b k) -> p b k", k=L)
        qis = sb("qis", [HD, NB, 32])
        wx = sb("wx", [NB, 2, P]); wm = sb("wm", [P, 2, NB])
        rs = sb("rs", [P, 2, L]); works = sb("works", [NB, L]); bias_s = sb("bias_s", [NB, L])
        tops = sb("tops", [NB, 8])
        qs = sb("qs", [P, NB, P]); kTs = sb("kTs", [P, 4, NB])
        caches = sb("caches", [P, CSLOTS * 4 * L])
        cring = [caches[:, i * 4 * L:(i + 1) * 4 * L] for i in range(CSLOTS)]
        st = caches[:, 0:2048]
        ps_s = rs
        mxs = sb("mxs", [P, 2]); nms = sb("nms", [P, 2]); sms = sb("sms", [P, 2]); ris = sb("ris", [P, 2])
        vrep = gate[:, 0:2, :]
        pts = gate[:, 2, :].rearrange("p (i n) -> p i n", n=P)
        qr = sb("qr", [P, 32]); kr = sb("kr", [P, 32]); vr = sb("vr", [P, HD])
        op = sb("op", [P, HD]); op2 = caches[0:NB, 2048:3072].rearrange("p (h j e) -> p h j e", h=NH, j=2); o_s = s_sb[1][0:NB]
        gcol = sb("gcol", [P, 4, KD]); gret = sb("gret", [P, W])
        cosT = sb("cosT", [P, TILES, HD]); sinT = sb("sinT", [P, TILES, HD])
        dm = sb("dm", [P, NH, P]); kdec = sb("kdec", [P, NH]); qdec = sb("qdec", [P, 4, P])
        cdec = sb("cdec", [P, 4]); gam = sb("gam", [P, 1])
        idn = sb("idn", [P, P]); exps = sb("exps", [NB, 2, P]); sel = sb("sel", [P, 2, NB])
        dg = sb("dg", [P, NH]); ones = sb("ones", [P, P]); eps = sb("eps", [P, 1])
        pg = sb("pg", [1, NB * NPAGES], I32)
        ps = ctx.enter_context(nc.psum_tensor("ps", [P, 8, 512], F32))

        def sem(name):
            return ctx.enter_context(nc.semaphore(name))

        const_in = sem("const_in"); zeroed = sem("zeroed"); layer_go = sem("layer_go"); y_out = sem("y_out")
        gains_in = sem("gains_in")
        kidx_in = sem("kidx_in")
        state_in = sem("state_in")
        sq_ready = sem("sq_ready")
        sq_used = sem("sq_used")
        ssum_ready = sem("ssum_ready")
        stat_mm = sem("stat_mm")
        std_ready = sem("std_ready")
        rstd_ready = sem("rstd_ready")
        rtok_mm = sem("rtok_mm")
        h_ready = sem("h_ready")
        proj_done = sem("proj_done")
        proj_read = sem("proj_read")
        rope_done = sem("rope_done")
        tr_mm = sem("tr_mm")
        tr_read = sem("tr_read")
        ts_mm = sem("ts_mm")
        ts_read = sem("ts_read")
        dot_mm = sem("dot_mm")
        dot_read = sem("dot_read")
        comb_done = sem("comb_done")
        sdot_mm = sem("sdot_mm")
        srelu_done = sem("srelu_done")
        wx_ready = sem("wx_ready")
        wm_mm = sem("wm_mm")
        wm_ready = sem("wm_ready")
        ssc_mm = sem("ssc_mm")
        ssc_read = sem("ssc_read")
        sbias_ready = sem("sbias_ready")
        bias_ready = sem("bias_ready")
        knew_done = sem("knew_done")
        cache_used = sem("cache_used")
        smx_ready = sem("smx_ready")
        sp_exp = sem("sp_exp")
        sp_ready = sem("sp_ready")
        spt_mm = sem("spt_mm")
        spt_ready = sem("spt_ready")
        vrep_mm = sem("vrep_mm")
        vrep_ready = sem("vrep_ready")
        om_ready = sem("om_ready")
        as_mm = sem("as_mm")
        as_read = sem("as_read")
        qz_ready = sem("qz_ready")
        att_mm = sem("att_mm")
        att_read = sem("att_read")
        p_exp = sem("p_exp")
        p_ready = sem("p_ready")
        pt_mm = sem("pt_mm")
        pt_ready = sem("pt_ready")
        pv_mm = sem("pv_mm")
        blk_read = sem("blk_read")
        gate_exp = sem("gate_exp")
        gate_ready = sem("gate_ready")
        ra_mm = sem("ra_mm")
        attm_ready = sem("attm_ready")
        qtd_ready = sem("qtd_ready")
        su_mm = sem("su_mm")
        sbd_ready = sem("sbd_ready")
        o_mm = sem("o_mm")
        o_read = sem("o_read")
        kbd_ready = sem("kbd_ready")
        bounce = sem("bounce")
        bounce_o = sem("bounce_o")
        sret_ready = sem("sret_ready")
        gvar_ready = sem("gvar_ready")
        gstd_ready = sem("gstd_ready")
        b_ready = sem("b_ready")
        bt_mm = sem("bt_mm")
        bt_read = sem("bt_read")
        mt_done = sem("mt_done")
        wo_read = sem("wo_read")
        up_read = sem("up_read")
        dn0_read = sem("dn0_read")
        dn1_read = sem("dn1_read")
        f_ready = sem("f_ready")
        x_ready = sem("x_ready")
        out_ki = sem("out_ki")
        out_k = sem("out_k")
        out_v = sem("out_v")
        out_r = sem("out_r")
        sopart = sem("sopart")
        ended = sem("ended")
        act_step = sem("act_step")
        dve_step = sem("dve_step")
        pool_step = sem("pool_step")
        w_slot = [sem(f"w_slot{i}") for i in range(SLOTS)]
        c_slot = [sem(f"c_slot{i}") for i in range(CSLOTS)]
        cleared = range(gains_in.num, c_slot[-1].num + 1)

        block = ctx.enter_context(nc.Block())

        def next_layer(eng, l):
            eng.drain().then_inc(ended, 1)
            eng.wait_ge(layer_go, l + 1)

        def unit_used(u):
            if u < U_PROJ:
                return proj_done, TILES * (u // 2 + 1)
            u -= U_PROJ
            if u < U_OUT:
                return mt_done, 2 * (u + 1)
            u -= U_OUT
            half, u = divmod(u, 2 * U_UP)
            base = KD + half * (FT + KD)
            return mt_done, base + (2 * (u + 1) if u < U_UP else FT + u - U_UP + 1)

        def mt_free(n):
            n -= 2
            if n < KD:
                return wo_read, n + 1
            half, j = divmod(n - KD, FT + KD)
            if j < FT:
                return up_read, half * FT + j + 1
            return (dn0_read if half == 0 else dn1_read), j - FT + 1

        @block.sync
        def _(sp):
            loads = [(x_feat[:], x), (cosT[:], tab_cos), (sinT[:], tab_sin), (dm[:], dmask), (kdec[:], k_decay),
                     (qdec[:], q_decay), (cdec[:], c_decay), (gam[:], s_gamma), (idn[:], ident), (exps[:], expand),
                     (sel[:], select), (dg[:], diag), (bias[:, 0:P], causal), (pg[:], pages)]
            for dst, src in loads:
                sp.dma_start(dst, src).then_inc(const_in, 16)
            sp.wait_ge(const_in, 16 * len(loads))
            page = [sp.value_load(pg[0:1, i:i + 1], min_val=0, max_val=cache_k.shape[1] - 1)
                    for i in range(NB * NPAGES)]
            with sp.Fori(0, DEPTH) as l:
                def layer(a, pat):
                    return a[bass.ds(l, 1)].rearrange(pat)

                sp.dma_start(gcol[:], layer(gains, "a p k n -> (a p) k n")).then_inc(gains_in, 16)
                sp.dma_start(gret[:], g_ret[bass.ds(l, 1)].to_broadcast([P, W])).then_inc(gains_in, 16)

                def unit(u):
                    if u >= SLOTS:
                        sm, v = unit_used(u - SLOTS)
                        sp.wait_ge(sm, v)
                    if u < 2:
                        src = w_idx[bass.ds(l, 1), u:u + 1].rearrange("a b p n -> (a b p) n")
                        sp.dma_start(wring[u % SLOTS][:, 0:4 * W_IDX], src).then_inc(w_slot[u % SLOTS], 16)
                    else:
                        src = w_all[bass.ds(l, 1), u - 2:u - 1].rearrange("a b p n -> (a b p) n")
                        sp.dma_start(wring[u % SLOTS][:], src).then_inc(w_slot[u % SLOTS], 16)

                def cache_tile(i):
                    if i >= CSLOTS:
                        sp.wait_ge(cache_used, i - CSLOTS + 1)
                    c, b = cring[i % CSLOTS], i % NB
                    for j in range(NPAGES):
                        pid = page[b * NPAGES + j]
                        if i < NB:
                            src = cache_k[bass.ds(l, 1), bass.ds(pid, 1)].rearrange("a b (h p) k -> p (a b h) k", p=P)
                            dst = c[:].rearrange("p (h k) -> p h k", k=L)[:, :, j * PAGE:(j + 1) * PAGE]
                        else:
                            src = cache_v[bass.ds(l, 1), bass.ds(pid, 1)].rearrange("a b k n -> (a b k) n")
                            dst = c[:, j * W:(j + 1) * W]
                        sp.dma_start(dst, src).then_inc(c_slot[i % CSLOTS], 16)

                for u in range(4):
                    unit(u)
                for b in range(NB):
                    for j in range(NPAGES):
                        src = cache_ki[bass.ds(l, 1), bass.ds(page[b * NPAGES + j], 1)].rearrange("a b d k -> (a b d) k")
                        sp.dma_start(kit[:, b, j * PAGE:(j + 1) * PAGE], src).then_inc(kidx_in, 16)
                for u in range(4, 10):
                    unit(u)
                for i in range(CSLOTS):
                    cache_tile(i)
                for u in range(10, 12):
                    unit(u)
                for i in range(CSLOTS, 2 * NB):
                    cache_tile(i)
                sp.wait_ge(cache_used, 2 * NB)
                sp.dma_start(st, layer(state, "a p n -> (a p) n")).then_inc(state_in, 16)
                for u in range(12, UNITS):
                    unit(u)
                sp.drain().then_inc(ended, 1)
                sp.wait_ge(ended, 5)
                sp.sem_clear(cleared)
                sp.sem_inc(layer_go, 1)
            sp.dma_start(y, x_feat[:]).then_inc(y_out, 16)
            sp.wait_ge(y_out, 16)

        @block.tensor
        def _(pe):
            mm = nc.tensor.matmul
            pe.wait_ge(const_in, 16 * 14)
            pe.wait_ge(zeroed, 1)

            def unit_here(u):
                pe.wait_ge(w_slot[u % SLOTS], 16 * (u // SLOTS + 1))

            def stats(n):
                pe.wait_ge(ssum_ready, n)
                for h in range(2):
                    last = mm(ps[:, 4 + h, 0:HALF], ones[:], ssum[:, h * HALF:(h + 1) * HALF], start=True, stop=True)
                last.then_inc(stat_mm, 1)

            def project(c):
                width = W if c else W_IDX
                for t in range(TILES):
                    n = c * TILES + t
                    if t == 0:
                        unit_here(2 * c)
                        unit_here(2 * c + 1)
                    if n >= 4:
                        pe.wait_ge(proj_read, n - 3)
                    for k in range(KD):
                        wt = wring[(2 * c + k // 4) % SLOTS][:, (k % 4) * width:(k % 4 + 1) * width]
                        last = mm(ps[0:rows(t), n % 4, 0:width], h_feat[:, k, token_cols(t)], wt,
                                  start=(k == 0), stop=(k == KD - 1))
                    last.then_inc(proj_done, 1)

            tg = [0]

            def transpose_groups(r, cols, sample):
                pe.wait_ge(rope_done, TILES * (r + 1))
                z = zr[r % 2]
                for c0, c1 in cols:
                    if tg[0] >= 2:
                        pe.wait_ge(tr_read, tg[0] - 1)
                    for t in range(NT):
                        last = nc.tensor.transpose(ps[0:c1 - c0, 4 + tg[0] % 2, t * P:(t + 1) * P],
                                                   z[:, t, c0:c1], idn[:])
                    last.then_inc(tr_mm, 1)
                    tg[0] += 1
                if sample:
                    for i, (c0, c1) in enumerate(sample):
                        last = nc.tensor.transpose(ps[0:c1 - c0, 7, i * NB:(i + 1) * NB], z[0:NB, NT, c0:c1],
                                                   idn[0:NB, 0:NB])
                    last.then_inc(ts_mm, 1)

            pairs = [(i * P, (i + 1) * P) for i in range(4)]
            heads = [(i * HD, (i + 1) * HD) for i in range(NI + 1)]

            with pe.Fori(0, DEPTH) as l:
                tg[0] = 0
                stats(1)
                pe.wait_ge(rstd_ready, 1)
                for t in range(TILES):
                    last = mm(ps[0:rows(t), 6, t:t + 1], rstd[0][:, token_cols(t)], idn[:, 0:1], start=True, stop=True)
                last.then_inc(rtok_mm, 1)
                pe.wait_ge(h_ready, KD)
                project(0)
                project(1)
                transpose_groups(0, [(0, P), (P, 2 * P), (2 * P, 2 * P + HD)], heads)
                pe.wait_ge(tr_read, 3)
                for j in range(3 * NI):
                    b, h = 1 + j // NI, j % NI
                    if j >= 2:
                        pe.wait_ge(dot_read, j - 1)
                    mm(ps[:, 4 + j % 2, 0:(b + 1) * P], qiT[:, h // 2, b * P:(b + 1) * P], kiz[h % 2][:, 0:b + 1, :],
                       start=True, stop=True).then_inc(dot_mm, 1)
                pe.wait_ge(kidx_in, 16 * NB * NPAGES)
                pe.wait_ge(ts_read, 1)
                pe.wait_ge(dot_read, 3 * NI)
                for b in range(NB):
                    last = mm(ps[32 * (b % 4):32 * (b % 4) + 32, 4 + b // 4, 0:L], qis[:, b, :], kit[:, b, :],
                              start=True, stop=True)
                last.then_inc(sdot_mm, 1)
                project(2)
                pe.wait_ge(wx_ready, 1)
                for g in range(2):
                    last = nc.tensor.transpose(ps[:, 6, 64 + g * NB:64 + (g + 1) * NB], wx[:, g, :], idn[0:NB, 0:NB])
                last.then_inc(wm_mm, 1)
                pe.wait_ge(wm_ready, 1)
                pe.wait_ge(srelu_done, 1)
                for g in range(2):
                    last = mm(ps[0:NB, 6, P:P + L], wm[:, g, :], rs[:, g, :], start=(g == 0), stop=(g == 1))
                last.then_inc(ssc_mm, 1)
                transpose_groups(1, pairs, pairs)
                project(3)
                pe.wait_ge(ts_read, 2)
                transpose_groups(2, pairs, pairs)
                pe.wait_ge(ssc_read, 1)
                pe.wait_ge(ts_read, 3)
                for g in range(2):
                    last = mm(ps[:, 6 + g, 0:W], exps[:, g, :], v_tok[0:NB, NT, :], start=True, stop=True)
                last.then_inc(vrep_mm, 1)
                project(4)
                pe.wait_ge(sbias_ready, 1)
                pe.wait_ge(tr_read, 11)
                for b in range(NB):
                    g, q4 = b // 4, 32 * (b % 4)
                    if b % 4 == 0:
                        mm(ps[:, 4 + g, 0:L], exps[:, g, :], bias_s[:], start=True, stop=False, skip_group_check=True)
                    pe.wait_ge(c_slot[b % CSLOTS], 16 * NPAGES * (b // CSLOTS + 1))
                    pe.wait_ge(knew_done, b + 1)
                    kc = cring[b % CSLOTS][:].rearrange("p (h k) -> p h k", k=L)
                    for h in range(4):
                        last = mm(ps[q4:q4 + 32, 4 + g, 0:L], qs[:, b, 32 * h:32 * h + 32], kc[:, h, :],
                                  start=False, stop=(h == 3), skip_group_check=True)
                    last.then_inc(cache_used, 1)
                project(5)
                pe.wait_ge(sp_ready, 2)
                pe.wait_ge(vrep_ready, 2)
                for i in range(4):
                    last = nc.tensor.transpose(ps[:, 6, i * P:(i + 1) * P],
                                               ps_s[:, i // 2, (i % 2) * PAGE:(i % 2 + 1) * PAGE], idn[:])
                last.then_inc(spt_mm, 1)
                pe.wait_ge(spt_ready, 1)
                for b in range(NB):
                    g, q4, i = b // 4, 32 * (b % 4), NB + b
                    pe.wait_ge(c_slot[i % CSLOTS], 16 * NPAGES * (i // CSLOTS + 1))
                    for j in range(NPAGES):
                        last = mm(ps[q4:q4 + 32, 4 + g, 0:W], pts[:, 2 * g + j, q4:q4 + 32],
                                  cring[i % CSLOTS][:, j * W:(j + 1) * W], start=(j == 0), stop=(j == 1))
                    last.then_inc(cache_used, 1)

                def scores(i):
                    b, h = divmod(i, NH)
                    if h == 0:
                        pe.wait_ge(qz_ready, b + 1)
                    if i == 0:
                        pe.wait_ge(om_ready, 2)
                    if i >= 2:
                        pe.wait_ge(att_read, i - 1)
                    mm(ps[:, 4 + i % 2, 0:(b + 1) * P], qz[b % 2][:, h, :], kT[:, h // 2, 0:(b + 1) * P],
                       start=True, stop=True).then_inc(att_mm, 1)

                def turn(i):
                    b = i // NH
                    pe.wait_ge(p_ready, i + 1)
                    if i >= 2:
                        pe.wait_ge(pt_ready, i - 1)
                    else:
                        pe.wait_ge(proj_read, 6 * TILES)
                    for j in range(b + 1):
                        last = nc.tensor.transpose(ps[:, i % 2, j * P:(j + 1) * P], p_sb[i % 2][:, j * P:(j + 1) * P], idn[:])
                    last.then_inc(pt_mm, 1)

                def values(i):
                    b, h = divmod(i, NH)
                    pe.wait_ge(pt_ready, i + 1)
                    if h == 0 and b >= 2:
                        pe.wait_ge(blk_read, b - 1)
                    r = HD * (h % 2)
                    for j in range(b + 1):
                        last = mm(ps[r:r + HD, 2 + b % 2, (h // 2) * P:(h // 2 + 1) * P],
                                  v_tok[:, j, h * HD:(h + 1) * HD], pt_sb[i % 2][:, j * P:(j + 1) * P],
                                  start=(j == 0), stop=(j == b))
                    last.then_inc(pv_mm, 1)

                for i in range(NT * NH + 2):
                    if i < NT * NH:
                        scores(i)
                    if 1 <= i <= NT * NH:
                        turn(i - 1)
                    if i >= 2:
                        values(i - 2)
                pe.wait_ge(om_ready, 2)
                for h in range(4):
                    for g in range(2):
                        last = mm(ps[:, 7, h * NB:(h + 1) * NB], vrep[:, g, h * P:(h + 1) * P], sel[:, g, :],
                                  start=(g == 0), stop=(g == 1))
                last.then_inc(as_mm, 1)
                pe.wait_ge(blk_read, NT)
                pe.wait_ge(pt_ready, NT * NH)
                project(6)
                project(7)
                pe.wait_ge(att_read, NT * NH)
                transpose_groups(3, pairs, None)
                transpose_groups(4, pairs, None)
                pe.wait_ge(tr_read, 19)
                pe.wait_ge(proj_read, 8 * TILES)
                for c in range(NT):
                    blk = slice(c * P, (c + 1) * P)
                    pe.wait_ge(qz_ready, NT + c + 1)
                    for g in range(2):
                        if c:
                            pe.wait_ge(attm_ready, 2 * (c - 1) + g + 1)
                        for h in range(4 * g, 4 * g + 4):
                            last = mm(ps[:, 4 + g, (h % 4) * P:(h % 4 + 1) * P], kT[:, h // 2, blk], qz[c % 2][:, h, :],
                                      start=True, stop=True)
                        last.then_inc(ra_mm, 1)
                    if c == 0:
                        pe.wait_ge(kbd_ready, NT)
                    else:
                        pe.wait_ge(sbd_ready, c)
                    kd = kbd[:, c, :]
                    for h in range(4):
                        last = mm(ps[:, 2, h * P:(h + 1) * P], kd[:, h * P:(h + 1) * P],
                                  v_tok[:, c, h * P:(h + 1) * P], start=True, stop=True)
                    last.then_inc(su_mm, 1)
                    pe.wait_ge(attm_ready, 2 * c + 2)
                    if c >= 2:
                        pe.wait_ge(o_read, c - 1)
                    if c:
                        pe.wait_ge(qtd_ready, c)
                    for h in range(4):
                        if c:
                            mm(ps[:, c % 2, h * P:(h + 1) * P], qTd[:, h, :], s_bd[:, h, :], start=True, stop=False)
                        for e in (2 * h, 2 * h + 1):
                            last = mm(ps[:, c % 2, e * HD:(e + 1) * HD], attm[:, e, :], v_tok[:, c, e * HD:(e + 1) * HD],
                                      start=(c == 0), stop=(c == 0 or e % 2 == 1))
                    last.then_inc(o_mm, 1)
                pe.wait_ge(attm_ready, 2 * NT)
                for t in range(TILES):
                    pe.wait_ge(b_ready, t + 1)
                    if t >= 2:
                        pe.wait_ge(bt_read, t - 1)
                    for h in range(4):
                        r = rows(t)
                        last = nc.tensor.transpose(ps[:, 4 + t % 2, h * r:(h + 1) * r], zr[1][0:r, t, h * P:(h + 1) * P],
                                                   idn[0:r, 0:r])
                    last.then_inc(bt_mm, 1)
                pe.wait_ge(bt_read, TILES)
                pe.wait_ge(as_read, 1)
                pe.wait_ge(o_read, NT)

                n = [0]

                def mtile(u, off, nk, src, first_wait=None):
                    i = n[0]
                    if i >= 2:
                        sm, v = mt_free(i)
                        pe.wait_ge(sm, v)
                    b0 = 2 * (i % 2)
                    wt = wring[u % SLOTS]
                    for k in range(nk):
                        if first_wait:
                            pe.wait_ge(first_wait[0], first_wait[1] + k + 1)
                        for h in range(2):
                            last = mm(ps[:, b0 + h, 0:HALF], wt[:, (off + k) * P:(off + k + 1) * P],
                                      src[:, k, h * HALF:(h + 1) * HALF], start=(k == 0), stop=(k == nk - 1))
                    last.then_inc(mt_done, 1)
                    n[0] += 1

                u = U_PROJ
                for j in range(U_OUT):
                    unit_here(u)
                    mtile(u, 0, KD, mix)
                    mtile(u, KD, KD, mix)
                    u += 1
                stats(2)
                for half in range(2):
                    for j in range(U_UP):
                        unit_here(u)
                        mtile(u, 0, KD, h_feat, (h_ready, KD) if half == 0 and j == 0 else None)
                        mtile(u, KD, KD, h_feat)
                        if half == 0 and j == 0:
                            stats(3)
                        u += 1
                    for j in range(KD):
                        unit_here(u)
                        mtile(u, 0, FT, ff, (f_ready, half * FT) if j == 0 else None)
                        u += 1
                stats(4)
                next_layer(pe, l)

        @block.scalar
        def _(act):
            act.wait_ge(const_in, 16 * 14)
            act.wait_ge(zeroed, 1)
            counts, up = counter()

            def squares(k, src):
                i = counts.get(sq_ready.num, 0)
                if i >= 3:
                    n, j = divmod(i - 3, KD)
                    if j == KD - 1:
                        act.wait_ge(ssum_ready, n + 1)
                    else:
                        act.wait_ge(sq_used, (KD - 2) * n + max(j, 1))
                nc.scalar.activation(sqr[i % 3][:], src, ACT.Square).then_inc(sq_ready, 1)
                act.wait_ge(sq_ready, up(sq_ready))

            def deviation(n):
                act.wait_ge(stat_mm, n)
                nc.scalar.activation(std[:].rearrange("p (b n) -> p b n", b=2), ps[:, 4:6, 0:HALF], ACT.Sqrt,
                                         bias=eps[:], scale=1.0 / D).then_inc(std_ready, 1)
                act.wait_ge(std_ready, up(std_ready))

            def evacuate(c):
                for t in range(TILES):
                    i, r = c * TILES + t, rows(t)
                    act.wait_ge(proj_done, i + 1)
                    src = ps[0:r, i % 4, 0:W if c else W_IDX]
                    if c in (3, 6):
                        dst, sc = v_tok[0:r, t, :], 0
                    elif c == 7:
                        dst, sc = gate[0:r, t, :], 0
                    else:
                        j = {0: 0, 1: 1, 2: 2, 4: 3, 5: 4}[c]
                        m = j * TILES + t
                        if m >= 3:
                            act.wait_ge(rope_done, m - 2)
                        dst, sc = raw[m % 3][0:r, 0:(W if c else W_IDX - NI)], (1 if c == 5 else 0)
                        if c == 0:
                            nc.scalar.activation(wi[0:r, t, :], src[:, W_IDX - NI:W_IDX], ACT.Copy, scale=rtok[0:r, 2, t:t + 1]).then_inc(act_step, 1)
                            act.wait_ge(act_step, up(act_step))
                            src = src[:, 0:W_IDX - NI]
                    nc.scalar.activation(dst, src, ACT.Copy, scale=rtok[0:r, sc, t:t + 1]).then_inc(proj_read, 1)
                    act.wait_ge(proj_read, up(proj_read))

            def take_groups(dsts):
                for d in dsts:
                    act.wait_ge(tr_mm, counts.get(tr_read.num, 0) + 1)
                    src = ps[:, 4 + counts.get(tr_read.num, 0) % 2, :]
                    if d is kiz:
                        keys = src[0:HD].rearrange("p (b n) -> p b n", n=P)
                        nc.scalar.activation(kiz[0][0:HD], keys, ACT.Copy).then_inc(act_step, 1)
                        act.wait_ge(act_step, up(act_step))
                        nc.scalar.activation(kiz[1][HD:P], keys, ACT.Copy).then_inc(tr_read, 1)
                        act.wait_ge(tr_read, up(tr_read))
                    else:
                        nc.scalar.activation(d, src, ACT.Copy).then_inc(tr_read, 1)
                        act.wait_ge(tr_read, up(tr_read))

            with act.Fori(0, DEPTH) as l:
                counts.clear()
                act.wait_ge(gains_in, 32)
                for k in range(KD):
                    squares(k, x_feat[:, k, :])
                deviation(1)
                for k in range(KD):
                    nc.scalar.activation(h_feat[:, k, :], x_feat[:, k, :], ACT.Copy, scale=gcol[:, 0, k:k + 1]).then_inc(h_ready, 1)
                    act.wait_ge(h_ready, up(h_ready))
                act.wait_ge(rtok_mm, 1)
                for j, f in enumerate((1.0, HD ** -0.5, NI ** -0.5 * HD ** -0.5)):
                    nc.scalar.mul(rtok[:, j, 0:NT], ps[:, 6, 0:NT], f).then_inc(act_step, 1)
                    act.wait_ge(act_step, up(act_step))
                    nc.scalar.mul(rtok[0:NB, j, NT:TILES], ps[0:NB, 6, NT:TILES], f).then_inc(act_step, 1)
                    act.wait_ge(act_step, up(act_step))
                evacuate(0)
                evacuate(1)
                take_groups([qiT[:, 0, :], qiT[:, 1, :], kiz])
                act.wait_ge(ts_mm, 1)
                nc.scalar.activation(qis[:, :, 0:NI], ps[0:HD, 7, 0:NI * NB].rearrange("p (h b) -> p b h", b=NB), ACT.Copy).then_inc(act_step, 1)
                act.wait_ge(act_step, up(act_step))
                nc.scalar.activation(kit[:, :, PAST], ps[0:HD, 7, NI * NB:(NI + 1) * NB], ACT.Copy).then_inc(ts_read, 1)
                act.wait_ge(ts_read, up(ts_read))
                act.dma_start(ki_out[bass.ds(l, 1)].rearrange("a (t p) n -> p (a t) n", p=P), zr[0][:, 0:NT, NI * HD:(NI + 1) * HD]).then_inc(out_ki, 16)
                act.dma_start(kis_out[bass.ds(l, 1)].rearrange("a p n -> (a p) n"), zr[0][0:NB, NT, NI * HD:(NI + 1) * HD]).then_inc(out_ki, 16)
                for j in range(3 * NI):
                    b = 1 + j // NI
                    act.wait_ge(dot_mm, j + 1)
                    if j >= 2:
                        act.wait_ge(comb_done, j - 1)
                    nc.scalar.activation(s_sb[j % 2][:, 0:(b + 1) * P], ps[:, 4 + j % 2, 0:(b + 1) * P], ACT.Relu).then_inc(dot_read, 1)
                    act.wait_ge(dot_read, up(dot_read))
                act.wait_ge(sdot_mm, 1)
                nc.scalar.activation(rs[:], ps[:, 4:6, 0:L], ACT.Relu).then_inc(srelu_done, 1)
                act.wait_ge(srelu_done, up(srelu_done))
                evacuate(2)
                act.wait_ge(wm_mm, 1)
                nc.scalar.activation(wm[:], ps[:, 6, 64:64 + 2 * NB].rearrange("p (g b) -> p g b", g=2), ACT.Copy).then_inc(wm_ready, 1)
                act.wait_ge(wm_ready, up(wm_ready))
                take_groups([qT[:, h, :] for h in range(4)])
                act.wait_ge(ts_mm, 2)
                q_s = ps[:, 7, 0:4 * NB].rearrange("p (h b) -> p b h", b=NB)
                nc.scalar.activation(qs[0:HD, :, 0:103:34], q_s[0:HD], ACT.Copy).then_inc(act_step, 1)
                act.wait_ge(act_step, up(act_step))
                nc.scalar.activation(qs[HD:P, :, 1:104:34], q_s[HD:P], ACT.Copy).then_inc(ts_read, 1)
                act.wait_ge(ts_read, up(ts_read))
                evacuate(3)
                act.dma_start(v_out[bass.ds(l, 1)].rearrange("a (t p) n -> p (a t) n", p=P), v_tok[:, 0:NT, :]).then_inc(out_v, 16)
                act.dma_start(vs_out[bass.ds(l, 1)].rearrange("a p n -> (a p) n"), v_tok[0:NB, NT, :]).then_inc(out_v, 16)
                take_groups([kT[:, h, :] for h in range(4)])
                act.wait_ge(ts_mm, 3)
                nc.scalar.activation(kTs[:], ps[:, 7, 0:4 * NB].rearrange("p (h b) -> p h b", b=NB), ACT.Copy).then_inc(ts_read, 1)
                act.wait_ge(ts_read, up(ts_read))
                act.dma_start(k_out[bass.ds(l, 1)].rearrange("a (t p) n -> p (a t) n", p=P), zr[0][:, 0:NT, :]).then_inc(out_k, 16)
                act.dma_start(ks_out[bass.ds(l, 1)].rearrange("a p n -> (a p) n"), zr[0][0:NB, NT, :]).then_inc(out_k, 16)
                act.wait_ge(vrep_mm, 1)
                for g in range(2):
                    nc.scalar.activation(vrep[:, g, :], ps[:, 6 + g, :], ACT.Copy).then_inc(vrep_ready, 1)
                    act.wait_ge(vrep_ready, up(vrep_ready))
                evacuate(4)
                for g in range(2):
                    act.wait_ge(smx_ready, g + 1)
                    nc.scalar.activation(ps_s[:, g, :], ps[:, 4 + g, 0:L], ACT.Exp, bias=nms[:, g:g + 1],
                                             scale=ATT_SCALE, accum_out=sms[:, g:g + 1]).then_inc(sp_exp, 1)
                    act.wait_ge(sp_exp, up(sp_exp))
                evacuate(5)
                act.wait_ge(spt_mm, 1)
                nc.scalar.activation(pts[:], ps[:, 6, :].rearrange("p (i n) -> p i n", n=P), ACT.Copy).then_inc(spt_ready, 1)
                act.wait_ge(spt_ready, up(spt_ready))
                for i in range(NT * NH + 1):
                    if i < NT * NH:
                        b = i // NH
                        act.wait_ge(att_read, i + 1)
                        if i >= 2:
                            act.wait_ge(pt_mm, i - 1)
                        nc.scalar.activation(p_sb[i % 2][:, 0:(b + 1) * P], s_sb[i % 2][:, 0:(b + 1) * P], ACT.Exp,
                                                 bias=neg_mx[:, i % 2:i % 2 + 1], scale=ATT_SCALE,
                                                 accum_out=rsum[:, i % 2:i % 2 + 1]).then_inc(p_exp, 1)
                        act.wait_ge(p_exp, up(p_exp))
                    if i >= 1:
                        j, b = i - 1, (i - 1) // NH
                        act.wait_ge(pt_mm, j + 1)
                        if j >= 2:
                            act.wait_ge(pv_mm, j - 1)
                        nc.scalar.activation(pt_sb[j % 2][:, 0:(b + 1) * P], ps[:, j % 2, 0:(b + 1) * P], ACT.Copy).then_inc(pt_ready, 1)
                        act.wait_ge(pt_ready, up(pt_ready))
                    if i >= 2 and (i - 1) % NH == 0:
                        b = (i - 1) // NH - 1
                        act.wait_ge(pv_mm, NH * (b + 1))
                        nc.scalar.activation(mix[:, 0:4, b * P:(b + 1) * P], ps[:, 2 + b % 2, :].rearrange("p (h n) -> p h n", h=4), ACT.Copy).then_inc(blk_read, 1)
                        act.wait_ge(blk_read, up(blk_read))
                act.wait_ge(pv_mm, NH * NT)
                nc.scalar.activation(mix[:, 0:4, 3 * P:SEQ], ps[:, 3, :].rearrange("p (h n) -> p h n", h=4), ACT.Copy).then_inc(blk_read, 1)
                act.wait_ge(blk_read, up(blk_read))
                act.wait_ge(as_mm, 1)
                nc.scalar.activation(mix[:, 0:4, SEQ:TOK], ps[:, 7, 0:4 * NB].rearrange("p (h b) -> p h b", b=NB), ACT.Copy).then_inc(as_read, 1)
                act.wait_ge(as_read, up(as_read))
                act.wait_ge(out_v, 32)
                evacuate(6)
                evacuate(7)
                take_groups([qT[:, h, :] for h in range(4)] + [kT[:, h, :] for h in range(4)])
                zq = zr[1][0:NB, NT, :].rearrange("b (r d) -> b r d", d=32)
                zk = zr[0][0:NB, NT, :].rearrange("b (r d) -> b r d", d=32)
                vv = v_tok[0:NB, NT, :].rearrange("b (r d) -> b r d", d=HD)
                act.dma_start(qr[:], zq).then_inc(bounce, 16)
                act.dma_start(kr[:], zk).then_inc(bounce, 16)
                for j in range(2):
                    act.dma_start(vr[j:P:2, :], vv).then_inc(bounce, 16)
                for t in range(TILES):
                    r = rows(t)
                    if t >= 2:
                        act.wait_ge(gate_ready, t - 1)
                    nc.scalar.activation(p_sb[t % 2][0:r], gate[0:r, t, :], ACT.Exp, scale=-1.0).then_inc(gate_exp, 1)
                    act.wait_ge(gate_exp, up(gate_exp))
                act.wait_ge(sopart, 1)
                act.dma_start(op2[:].rearrange("b h j e -> b (h j) e"), op[:]).then_inc(bounce_o, 16)
                act.wait_ge(sret_ready, 1)
                act.dma_start(rets_out[bass.ds(l, 1)].rearrange("a p n -> (a p) n"), st[:]).then_inc(out_r, 16)
                act.wait_ge(sbd_ready, NT)
                for e in range(2):
                    act.dma_start(ret_out[bass.ds(l, 1), e::2].rearrange("a h d e -> d (a h) e"),
                                  s_bd[HD * e:HD * e + HD, :, HD * e:HD * e + HD]).then_inc(out_r, 16)
                act.wait_ge(gvar_ready, 1)
                nc.scalar.activation(gn_var[:], gn_var[:], ACT.Sqrt, bias=eps[:], scale=1.0 / HD).then_inc(gstd_ready, 1)
                act.wait_ge(gstd_ready, up(gstd_ready))
                for t in range(TILES):
                    act.wait_ge(bt_mm, t + 1)
                    r = rows(t)
                    nc.scalar.activation(mix[:, 4:8, token_cols(t)], ps[:, 4 + t % 2, 0:4 * r].rearrange("p (h n) -> p h n", h=4), ACT.Copy).then_inc(bt_read, 1)
                    act.wait_ge(bt_read, up(bt_read))
                act.wait_ge(out_k, 32)
                for m in range(KD):
                    act.wait_ge(mt_done, m + 1)
                    nc.scalar.activation(osb[:, m, :].rearrange("p (b n) -> p b n", b=2), ps[:, 2 * (m % 2):2 * (m % 2) + 2, 0:HALF], ACT.Copy).then_inc(wo_read, 1)
                    act.wait_ge(wo_read, up(wo_read))
                    squares(m, osb[:, m, :])
                deviation(2)
                for k in range(KD):
                    act.wait_ge(x_ready, k + 1)
                    nc.scalar.activation(h_feat[:, k, :], x_feat[:, k, :], ACT.Copy, scale=gcol[:, 2, k:k + 1]).then_inc(h_ready, 1)
                    act.wait_ge(h_ready, up(h_ready))
                    squares(k, x_feat[:, k, :])
                deviation(3)
                for half in range(2):
                    for j in range(FT):
                        i = half * FT + j
                        act.wait_ge(up_read, i + 1)
                        nc.scalar.activation(ff[:, j, :], ff[:, j, :], ACT.Square).then_inc(f_ready, 1)
                        act.wait_ge(f_ready, up(f_ready))
                    for m in range(KD):
                        i = KD + half * (FT + KD) + FT + m
                        if half == 0:
                            act.wait_ge(mt_done, i + 1)
                            nc.scalar.activation(osb[:, m, :].rearrange("p (b n) -> p b n", b=2), ps[:, 2 * (i % 2):2 * (i % 2) + 2, 0:HALF], ACT.Copy).then_inc(dn0_read, 1)
                            act.wait_ge(dn0_read, up(dn0_read))
                        else:
                            act.wait_ge(dn1_read, m + 1)
                            squares(m, osb[:, m, :])
                deviation(4)
                act.wait_ge(out_ki, 32)
                act.wait_ge(out_r, 48)
                next_layer(act, l)

        @block.vector
        def _(dve):
            v = nc.vector
            dve.wait_ge(const_in, 16 * 14)
            v.memset(ones[:], 1.0)
            v.memset(eps[:], EPS)
            for q in qz:
                v.memset(q[:], 0.0)
            v.memset(s_bd[:], 0.0)
            v.memset(qis[:], 0.0)
            v.memset(qs[:], 0.0)
            v.memset(wx[:], 0.0)
            v.memset(gn_var[:], 1.0)
            dve.drain().then_inc(zeroed, 1)
            dve.wait_ge(zeroed, 1)
            counts, up = counter()

            def inverse(n):
                dve.wait_ge(std_ready, n)
                v.reciprocal(rstd[(n - 1) % 2][:], std[:]).then_inc(rstd_ready, 1)
                dve.wait_ge(rstd_ready, up(rstd_ready))

            def rope(j, c):
                z, nh = zr[j % 2], (NH if c else NI + 1)
                for t in range(TILES):
                    m, r = j * TILES + t, rows(t)
                    dve.wait_ge(proj_read, c * TILES + t + 1)
                    a = raw[m % 3][0:r, 0:nh * HD].rearrange("p (h d) -> p h d", d=HD)
                    t1 = rt[0][0:r, 0:nh * HD].rearrange("p (h d) -> p h d", d=HD)
                    t2 = rt[1][0:r, 0:nh * HD].rearrange("p (h d) -> p h d", d=HD)
                    cs = cosT[0:r, t:t + 1, :].to_broadcast([r, nh, HD])
                    sn = sinT[0:r, t:t + 1, :].to_broadcast([r, nh, HD])
                    v.tensor_tensor(t1, a, cs, ALU.mult).then_inc(dve_step, 1)
                    dve.wait_ge(dve_step, up(dve_step))
                    v.tensor_tensor(t2[:, :, 0:32], a[:, :, 32:64], sn[:, :, 0:32], ALU.mult).then_inc(dve_step, 1)
                    dve.wait_ge(dve_step, up(dve_step))
                    v.tensor_tensor(t2[:, :, 32:64], a[:, :, 0:32], sn[:, :, 32:64], ALU.mult).then_inc(dve_step, 1)
                    dve.wait_ge(dve_step, up(dve_step))
                    v.tensor_tensor(z[0:r, t, 0:nh * HD], rt[0][0:r, 0:nh * HD], rt[1][0:r, 0:nh * HD], ALU.add).then_inc(rope_done, 1)
                    dve.wait_ge(rope_done, up(rope_done))

            def select_top(w, t8, n):
                for _ in range(n // 8):
                    v.max(t8, w).then_inc(dve_step, 1)
                    dve.wait_ge(dve_step, up(dve_step))
                    v.match_replace(w, t8, w, MARK).then_inc(dve_step, 1)
                    dve.wait_ge(dve_step, up(dve_step))

            def update(g, n):
                for k in range(KD):
                    v.scalar_tensor_tensor(upd[:], osb[:, k, :], gcol[:, g, k:k + 1], rstd[(n - 1) % 2][:], ALU.mult, ALU.mult).then_inc(dve_step, 1)
                    dve.wait_ge(dve_step, up(dve_step))
                    v.tensor_tensor(x_feat[:, k, :], x_feat[:, k, :], upd[:], ALU.add).then_inc(x_ready, 1)
                    dve.wait_ge(x_ready, up(x_ready))

            with dve.Fori(0, DEPTH) as l:
                counts.clear()
                inverse(1)
                rope(0, 0)
                wv = wi[0:NB, NT:TILES, :]
                v.tensor_tensor(wx[:].rearrange("b g (q h) -> b (g q) h", h=32)[:, :, 0:NI],
                                    exps[:].rearrange("b g (q h) -> b (g q) h", h=32)[:, :, 0:NI],
                                    wv.to_broadcast([NB, NB, NI]), ALU.mult).then_inc(wx_ready, 1)
                dve.wait_ge(wx_ready, up(wx_ready))
                rope(1, 1)
                sc = {1: bias[:, 128:384], 2: bias[:, 384:768], 3: bias[:, 768:1280]}
                for j in range(3 * NI):
                    b, h = 1 + j // NI, j % NI
                    dve.wait_ge(dot_read, j + 1)
                    r = s_sb[j % 2][:, 0:(b + 1) * P]
                    if h == 0:
                        v.tensor_scalar(sc[b], r, wi[:, b, 0:1], None, ALU.mult).then_inc(comb_done, 1)
                        dve.wait_ge(comb_done, up(comb_done))
                    else:
                        v.scalar_tensor_tensor(sc[b], r, wi[:, b, h:h + 1], sc[b], ALU.mult, ALU.add).then_inc(comb_done, 1)
                        dve.wait_ge(comb_done, up(comb_done))
                    if h == NI - 1:
                        v.tensor_tensor(sc[b][:, b * P:(b + 1) * P], sc[b][:, b * P:(b + 1) * P], bias[:, 0:P], ALU.add).then_inc(dve_step, 1)
                        dve.wait_ge(dve_step, up(dve_step))
                dve.wait_ge(out_ki, 32)
                dve.wait_ge(tr_mm, 3)
                dve.wait_ge(ts_mm, 1)
                rope(2, 2)
                dve.wait_ge(ssc_mm, 1)
                v.tensor_copy(works[:], ps[0:NB, 6, P:P + L]).then_inc(ssc_read, 1)
                dve.wait_ge(ssc_read, up(ssc_read))
                select_top(works[:], tops[:], TOPK_S)
                v.tensor_scalar(bias_s[:], works[:], MARK, NEG, ALU.not_equal, ALU.mult).then_inc(sbias_ready, 1)
                dve.wait_ge(sbias_ready, up(sbias_ready))
                for b in range(1, NT):
                    select_top(sc[b], top8[:], TOPK_P)
                    v.tensor_scalar(sc[b], sc[b], MARK, NEG, ALU.not_equal, ALU.mult).then_inc(bias_ready, 1)
                    dve.wait_ge(bias_ready, up(bias_ready))
                dve.wait_ge(tr_mm, 7)
                rope(3, 4)
                for g in range(2):
                    dve.wait_ge(cache_used, 4 * g + 4)
                    v.reduce_max(mxs[:, g:g + 1], ps[:, 4 + g, 0:L], AX_X).then_inc(dve_step, 1)
                    dve.wait_ge(dve_step, up(dve_step))
                    v.tensor_scalar(nms[:, g:g + 1], mxs[:, g:g + 1], -ATT_SCALE, None, ALU.mult).then_inc(smx_ready, 1)
                    dve.wait_ge(smx_ready, up(smx_ready))
                for g in range(2):
                    dve.wait_ge(sp_exp, g + 1)
                    v.reciprocal(ris[:, g:g + 1], sms[:, g:g + 1]).then_inc(dve_step, 1)
                    dve.wait_ge(dve_step, up(dve_step))
                    v.tensor_scalar(ps_s[:, g, :], ps_s[:, g, :], ris[:, g:g + 1], None, ALU.mult).then_inc(sp_ready, 1)
                    dve.wait_ge(sp_ready, up(sp_ready))
                dve.wait_ge(out_k, 32)
                dve.wait_ge(tr_mm, 11)
                dve.wait_ge(ts_mm, 3)
                rope(4, 5)
                for t in range(NT):
                    kd = kbd[:, t, :]
                    v.tensor_tensor(kd.rearrange("p (h d) -> p h d", d=HD), zr[0][:, t, :].rearrange("p (h d) -> p h d", d=HD),
                                        kdec[:].rearrange("p (h o) -> p h o", o=1).to_broadcast([P, NH, HD]), ALU.mult).then_inc(kbd_ready, 1)
                    dve.wait_ge(kbd_ready, up(kbd_ready))
                for g in range(2):
                    dve.wait_ge(cache_used, NB + 4 * g + 4)
                    dve.wait_ge(vrep_ready, g + 1)
                    v.scalar_tensor_tensor(vrep[:, g, :], vrep[:, g, :], ps_s[:, g, PAST:L], ps[:, 4 + g, :],
                                               ALU.mult, ALU.add).then_inc(dve_step, 1)
                    dve.wait_ge(dve_step, up(dve_step))
                    vg = vrep[:, g, :].rearrange("p (h d) -> p h d", d=HD)
                    v.tensor_tensor(vg, vg, dg[:].rearrange("p (h o) -> p h o", o=1).to_broadcast([P, NH, HD]), ALU.mult).then_inc(om_ready, 1)
                    dve.wait_ge(om_ready, up(om_ready))
                for i in range(NT * NH + 1):
                    if i < NT * NH:
                        b, c = i // NH, i % 2
                        n = (b + 1) * P
                        dve.wait_ge(att_mm, i + 1)
                        if i >= 2:
                            dve.wait_ge(p_exp, i - 1)
                        v.tensor_tensor_reduce(out=s_sb[c][:, 0:n], in0=ps[:, 4 + c, 0:n], in1=bias[:, b_at[b]:b_at[b] + n],
                                                   scale=1.0, scalar=-3e38, op0=ALU.add, op1=ALU.max, accum_out=mx[:, c:c + 1]).then_inc(dve_step, 1)
                        dve.wait_ge(dve_step, up(dve_step))
                        v.tensor_scalar(neg_mx[:, c:c + 1], mx[:, c:c + 1], -ATT_SCALE, None, ALU.mult).then_inc(att_read, 1)
                        dve.wait_ge(att_read, up(att_read))
                    if i >= 1:
                        j = i - 1
                        n, c = (j // NH + 1) * P, j % 2
                        dve.wait_ge(p_exp, j + 1)
                        v.reciprocal(rinv[:, c:c + 1], rsum[:, c:c + 1]).then_inc(dve_step, 1)
                        dve.wait_ge(dve_step, up(dve_step))
                        v.tensor_scalar(p_sb[c][:, 0:n], p_sb[c][:, 0:n], rinv[:, c:c + 1], None, ALU.mult).then_inc(p_ready, 1)
                        dve.wait_ge(p_ready, up(p_ready))
                for t in range(TILES):
                    r = rows(t)
                    dve.wait_ge(gate_exp, t + 1)
                    e = p_sb[t % 2][0:r]
                    v.tensor_scalar(e, e, 1.0, None, ALU.add).then_inc(dve_step, 1)
                    dve.wait_ge(dve_step, up(dve_step))
                    v.reciprocal(e, e).then_inc(dve_step, 1)
                    dve.wait_ge(dve_step, up(dve_step))
                    v.tensor_tensor(gate[0:r, t, :], gate[0:r, t, :], e, ALU.mult).then_inc(gate_ready, 1)
                    dve.wait_ge(gate_ready, up(gate_ready))
                dve.wait_ge(bounce, 64)
                dve.wait_ge(state_in, 16)
                stv = st[:].rearrange("p (d e) -> p d e", e=HD)
                for q in range(4):
                    d8 = slice(8 * q, 8 * q + 8)
                    tv = rt[0][:].rearrange("p (d e) -> p d e", e=HD)
                    v.tensor_tensor(tv, kr[:, d8].rearrange("p (d o) -> p d o", o=1).to_broadcast([P, 8, HD]),
                                        vr[:].rearrange("p (o e) -> p o e", o=1).to_broadcast([P, 8, HD]), ALU.mult).then_inc(dve_step, 1)
                    dve.wait_ge(dve_step, up(dve_step))
                    sq = st[:, 512 * q:512 * (q + 1)]
                    done = sret_ready if q == 3 else dve_step
                    v.scalar_tensor_tensor(sq, sq, gam[:], rt[0][:], ALU.mult, ALU.add).then_inc(done, 1)
                    dve.wait_ge(done, up(done))
                    v.tensor_tensor(tv, stv[:, d8, :], qr[:, d8].rearrange("p (d o) -> p d o", o=1).to_broadcast([P, 8, HD]), ALU.mult).then_inc(dve_step, 1)
                    dve.wait_ge(dve_step, up(dve_step))
                    dst = op[:] if q == 0 else rt[1][:, 0:HD]
                    v.tensor_reduce(dst, rt[0][:].rearrange("p (d e) -> p e d", e=HD), AX_X, ALU.add).then_inc(dve_step, 1)
                    dve.wait_ge(dve_step, up(dve_step))
                    if q:
                        done = sopart if q == 3 else dve_step
                        v.tensor_tensor(op[:], op[:], rt[1][:, 0:HD], ALU.add).then_inc(done, 1)
                        dve.wait_ge(done, up(done))

                oc = zr[1]

                def centre(t, o):
                    r = rows(t)
                    ov = o.rearrange("p (h d) -> p h d", d=HD)
                    v.tensor_reduce(gn_mu[0:r, t, :], ov, AX_X, ALU.add).then_inc(dve_step, 1)
                    dve.wait_ge(dve_step, up(dve_step))
                    v.tensor_scalar(gn_mu[0:r, t, :], gn_mu[0:r, t, :], 1.0 / HD, None, ALU.mult).then_inc(dve_step, 1)
                    dve.wait_ge(dve_step, up(dve_step))
                    v.tensor_tensor(oc[0:r, t, :].rearrange("p (h d) -> p h d", d=HD), ov,
                                        gn_mu[0:r, t, :].rearrange("p (h o) -> p h o", o=1).to_broadcast([r, NH, HD]), ALU.subtract).then_inc(o_read, 1)
                    dve.wait_ge(o_read, up(o_read))
                    v.tensor_tensor(rt[1][0:r], oc[0:r, t, :], oc[0:r, t, :], ALU.mult).then_inc(dve_step, 1)
                    dve.wait_ge(dve_step, up(dve_step))
                    done = gvar_ready if t == NT else dve_step
                    v.tensor_reduce(gn_var[0:r, t, :], rt[1][0:r].rearrange("p (h d) -> p h d", d=HD), AX_X, ALU.add).then_inc(done, 1)
                    dve.wait_ge(done, up(done))

                dve.wait_ge(tr_mm, 19)
                for c in range(NT):
                    for g in range(2):
                        dve.wait_ge(ra_mm, 2 * c + g + 1)
                        if c and g == 0:
                            dve.wait_ge(o_mm, c)
                        v.tensor_tensor(attm[:, 4 * g:4 * g + 4, :], ps[:, 4 + g, :].rearrange("p (h n) -> p h n", h=4),
                                            dm[:, 4 * g:4 * g + 4, :], ALU.mult).then_inc(attm_ready, 1)
                        dve.wait_ge(attm_ready, up(attm_ready))
                    dve.wait_ge(su_mm, c + 1)
                    dve.wait_ge(o_mm, c + 1)
                    su = ps[:, 2, :].rearrange("p (h n) -> p h n", h=4)
                    if c:
                        cd = cdec[:].rearrange("p (h o) -> p h o", o=1).to_broadcast([P, 4, HD])
                    for e in range(2):
                        rr, cc = slice(HD * e, HD * e + HD), slice(HD * e, HD * e + HD)
                        done = sbd_ready if e else dve_step
                        if c == 0:
                            v.tensor_copy(s_bd[rr, :, cc], su[rr, :, cc]).then_inc(done, 1)
                            dve.wait_ge(done, up(done))
                        else:
                            v.tensor_tensor(s_tmp[rr], s_bd[rr, :, cc], cd[rr], ALU.mult).then_inc(dve_step, 1)
                            dve.wait_ge(dve_step, up(dve_step))
                            v.tensor_tensor(s_bd[rr, :, cc], s_tmp[rr], su[rr, :, cc], ALU.add).then_inc(done, 1)
                            dve.wait_ge(done, up(done))
                    if c < NT - 1:
                        v.tensor_tensor(qTd[:], qT[:, :, (c + 1) * P:(c + 2) * P], qdec[:], ALU.mult).then_inc(qtd_ready, 1)
                        dve.wait_ge(qtd_ready, up(qtd_ready))
                    centre(c, ps[:, c % 2, :])
                dve.wait_ge(bounce_o, 16)
                dve.wait_ge(bounce, 64)
                v.tensor_tensor(o_s[:].rearrange("b (h e) -> b h e", e=HD), op2[:, :, 0, :], op2[:, :, 1, :], ALU.add).then_inc(dve_step, 1)
                dve.wait_ge(dve_step, up(dve_step))
                centre(NT, o_s[:])
                dve.wait_ge(gstd_ready, 1)
                v.reciprocal(gn_var[:], gn_var[:]).then_inc(dve_step, 1)
                dve.wait_ge(dve_step, up(dve_step))
                for t in range(TILES):
                    r = rows(t)
                    ocv = oc[0:r, t, :].rearrange("p (h d) -> p h d", d=HD)
                    v.tensor_tensor(ocv, ocv, gn_var[0:r, t, :].rearrange("p (h o) -> p h o", o=1).to_broadcast([r, NH, HD]), ALU.mult).then_inc(dve_step, 1)
                    dve.wait_ge(dve_step, up(dve_step))
                    v.tensor_tensor(oc[0:r, t, :], oc[0:r, t, :], gret[0:r, :], ALU.mult).then_inc(dve_step, 1)
                    dve.wait_ge(dve_step, up(dve_step))
                    v.tensor_tensor(oc[0:r, t, :], oc[0:r, t, :], gate[0:r, t, :], ALU.mult).then_inc(b_ready, 1)
                    dve.wait_ge(b_ready, up(b_ready))
                inverse(2)
                update(1, 2)
                inverse(3)
                for half in range(2):
                    for j in range(FT):
                        i = KD + half * (FT + KD) + j
                        dve.wait_ge(mt_done, i + 1)
                        if half and j == 0:
                            dve.wait_ge(mt_done, KD + FT + KD)
                        v.scalar_tensor_tensor(ff[:, j, :].rearrange("p (b n) -> p b n", b=2), ps[:, 2 * (i % 2):2 * (i % 2) + 2, 0:HALF],
                                                   0.0, rstd[0][:].rearrange("p (b n) -> p b n", b=2), ALU.max, ALU.mult).then_inc(up_read, 1)
                        dve.wait_ge(up_read, up(up_read))
                    if half:
                        for m in range(KD):
                            i = KD + FT + KD + FT + m
                            dve.wait_ge(mt_done, i + 1)
                            om = osb[:, m, :].rearrange("p (b n) -> p b n", b=2)
                            v.tensor_tensor(om, om, ps[:, 2 * (i % 2):2 * (i % 2) + 2, 0:HALF], ALU.add).then_inc(dn1_read, 1)
                            dve.wait_ge(dn1_read, up(dn1_read))
                inverse(4)
                update(3, 4)
                next_layer(dve, l)

        @block.gpsimd
        def _(pool):
            pool.wait_ge(zeroed, 1)
            counts, up = counter()

            def sum_squares(n):
                base = KD * (n - 1)
                if n > 1:
                    pool.wait_ge(stat_mm, n - 1)
                pool.wait_ge(sq_ready, base + 2)
                a, b = sqr[base % 3], sqr[(base + 1) % 3]
                nc.gpsimd.tensor_tensor(ssum[:], a[:], b[:], ALU.add).then_inc(sq_used, 1)
                pool.wait_ge(sq_used, up(sq_used))
                for k in range(2, KD):
                    pool.wait_ge(sq_ready, base + k + 1)
                    done = sq_used if k < KD - 1 else ssum_ready
                    nc.gpsimd.tensor_tensor(ssum[:], ssum[:], sqr[(base + k) % 3][:], ALU.add).then_inc(done, 1)
                    pool.wait_ge(done, up(done))

            def queries(b):
                blk = slice((b % 4) * P, (b % 4 + 1) * P)
                q = qz[b % 2]
                nc.gpsimd.tensor_copy(q[0:HD, 0:NH:2, :], qT[0:HD, :, blk]).then_inc(pool_step, 1)
                pool.wait_ge(pool_step, up(pool_step))
                nc.gpsimd.tensor_copy(q[HD:P, 1:NH:2, :], qT[HD:P, :, blk]).then_inc(qz_ready, 1)
                pool.wait_ge(qz_ready, up(qz_ready))

            with pool.Fori(0, DEPTH) as l:
                counts.clear()
                sum_squares(1)
                pool.wait_ge(ts_read, 3)
                pool.wait_ge(tr_read, 7)
                for b in range(NB):
                    if b >= CSLOTS:
                        pool.wait_ge(cache_used, b - CSLOTS + 1)
                    kc = cring[b % CSLOTS][:].rearrange("p (h k) -> p h k", k=L)
                    nc.gpsimd.tensor_copy(kc[:, :, PAST], kTs[:, :, b]).then_inc(knew_done, 1)
                    pool.wait_ge(knew_done, up(knew_done))
                for b in range(NT):
                    if b >= 2:
                        pool.wait_ge(att_mm, NH * (b - 1))
                    queries(b)
                pool.wait_ge(tr_read, 15)
                pool.wait_ge(att_mm, NH * NT)
                for c in range(NT):
                    if c >= 2:
                        pool.wait_ge(ra_mm, 2 * (c - 1))
                    queries(NT + c)
                for n in range(2, 5):
                    sum_squares(n)
                next_layer(pool, l)


def constants():
    f = np.float32
    half = HD // 2
    inv = (f(10000.0) ** (-np.arange(half, dtype=f) / f(half))).astype(f)
    pos = np.zeros((P, TILES), f)
    pos[:, 0:NT] = np.arange(SEQ, dtype=f).reshape(NT, P).T
    pos[:, NT] = PAST
    ang = (pos[:, :, None] * inv[None, None, :]).astype(f)
    c, s = np.cos(ang).astype(f), np.sin(ang).astype(f)
    lg = np.log1p(-np.exp2(-5.0 - np.arange(NH)))
    i = np.arange(P)
    diff = i[None, :] - i[:, None]
    dmask = np.where(diff[:, None, :] >= 0, np.exp(np.maximum(diff, 0)[:, None, :] * lg[None, :, None]), 0.0)
    pair = np.arange(P)[:, None] // HD + 2 * np.arange(4)[None, :]
    qdec = np.exp((i[None, None, :] + 1.0) * lg[pair][:, :, None])
    expand = np.zeros((NB, 2, P), f)
    for b in range(NB):
        expand[b, b // 4, 32 * (b % 4):32 * (b % 4) + 32] = 1.0
    diag = np.zeros((P, NH), f)
    for r in range(P):
        if r % 32 < NH:
            diag[r, r % 32] = 1.0
    return dict(
        tab_cos=np.concatenate([c, c], -1), tab_sin=np.concatenate([-s, s], -1), dmask=dmask.astype(f),
        k_decay=np.exp((P - 1.0 - i)[:, None] * lg[None, :]).astype(f), q_decay=qdec.astype(f),
        c_decay=np.exp(P * lg[pair]).astype(f),
        s_gamma=np.exp(lg[(np.arange(P) // 2) % NH]).astype(f)[:, None], ident=np.eye(P, dtype=f),
        expand=expand, select=np.ascontiguousarray(expand.transpose(2, 1, 0)), diag=diag,
        causal=np.where(i[None, :] <= i[:, None], 0.0, NEG).astype(f))


def kernel(x_prompt, x_sample, cache_k, cache_v, cache_kidx, state_ret, page_table, w_in, w_out, g_ret,
           g_mix_pre, g_mix_post, g_ffn_pre, g_ffn_post, w_up, w_down):
    import concourse.bacc as bacc
    from concourse.bass_utils import run_bass_kernel_spmd

    A = lambda a: np.asarray(a)
    x = np.concatenate([A(x_prompt).reshape(SEQ, D), A(x_sample).reshape(NB, D)])
    n_pool = cache_k.shape[1]
    w_in = A(w_in)
    a3, idx = 3 * W, W_IDX
    starts = [0, W, 2 * W, a3 + idx, a3 + idx + W, a3 + idx + 2 * W, a3 + idx + 3 * W]

    def moving(w):
        n = w.shape[-1]
        return w.reshape(DEPTH, 2, 4, P, n).transpose(0, 1, 3, 2, 4).reshape(DEPTH, 2, P, 4 * n)

    def stationary(w, kn, per):
        m = w.shape[-1] // P
        v = w.reshape(DEPTH, kn, P, m, P).transpose(0, 3, 2, 1, 4).reshape(DEPTH, m // per, per, P, kn * P)
        return v.transpose(0, 1, 3, 2, 4).reshape(DEPTH, m // per, P, per * kn * P)

    w_up, w_down = A(w_up), A(w_down)
    parts = [moving(w_in[:, :, c:c + W]) for c in starts] + [stationary(A(w_out), KD, 2)]
    for half in range(2):
        f0, f1 = half * FF // 2, (half + 1) * FF // 2
        parts += [stationary(w_up[:, :, f0:f1], KD, 2), stationary(w_down[:, f0:f1, :], FT, 1)]
    arrays = dict(
        x=x.T.reshape(KD, P, TOK).transpose(1, 0, 2),
        w_idx=moving(w_in[:, :, a3:a3 + idx]), w_all=np.concatenate(parts, 1),
        gains=np.stack([A(g).reshape(DEPTH, KD, P).transpose(0, 2, 1) for g in
                        (g_mix_pre, g_mix_post, g_ffn_pre, g_ffn_post)], 2),
        g_ret=A(g_ret),
        cache_k=A(cache_k).reshape(DEPTH, n_pool, PAGE, W).transpose(0, 1, 3, 2),
        cache_v=A(cache_v).reshape(DEPTH, n_pool, PAGE, W),
        cache_ki=A(cache_kidx).transpose(0, 1, 3, 2),
        state=A(state_ret).reshape(DEPTH, P, 2048),
        pages=A(page_table).astype(np.int32).reshape(1, NB * NPAGES), **constants())
    outs = dict(y=(P, KD, TOK), k_out=(DEPTH, SEQ, W), v_out=(DEPTH, SEQ, W), ki_out=(DEPTH, SEQ, HD),
                ret_out=(DEPTH, NH, HD, HD), ks_out=(DEPTH, NB, W), vs_out=(DEPTH, NB, W),
                kis_out=(DEPTH, NB, HD), rets_out=(DEPTH, P, 2048))
    nc = bacc.Bacc("TRN2", target_bir_lowering=False, num_devices=1, dynamic_dma_scratch_size=1024)
    args, given = {}, {}
    for name, a in arrays.items():
        a = np.ascontiguousarray(a)
        given[f"in_{name}"] = a
        args[name] = nc.dram_tensor(f"in_{name}", a.shape, mybir.dt.from_np(a.dtype), kind="ExternalInput").ap()
    for name, shape in outs.items():
        args[name] = nc.dram_tensor(f"o_{name}", shape, F32, kind="ExternalOutput").ap()
    build(nc, **args)
    r = run_bass_kernel_spmd(nc, [given], core_ids=[0]).results[0]
    o = {name: r[f"o_{name}"] for name in outs}
    yy = np.asarray(o["y"]).transpose(2, 1, 0).reshape(TOK, D)
    return (yy[0:SEQ].reshape(1, SEQ, D), yy[SEQ:].reshape(NB, 1, D),
            o["k_out"].reshape(DEPTH, 1, SEQ, NH, HD), o["v_out"].reshape(DEPTH, 1, SEQ, NH, HD),
            o["ki_out"].reshape(DEPTH, 1, SEQ, HD), o["ret_out"].reshape(DEPTH, 1, NH, HD, HD),
            o["ks_out"].reshape(DEPTH, NB, 1, NH, HD), o["vs_out"].reshape(DEPTH, NB, 1, NH, HD),
            o["kis_out"].reshape(DEPTH, NB, 1, HD), o["rets_out"].reshape(DEPTH, NB, NH, HD, HD))
```

```python
import numpy as np
import concourse.bass as bass
from concourse import mybir
from contextlib import ExitStack

F32 = mybir.dt.float32
I32 = mybir.dt.int32
ALU = mybir.AluOpType
ACT = mybir.ActivationFunctionType
AX_X = mybir.AxisListType.X

D = 1024
DEPTH = 2
SEQ = 512
NB = 8
PAGE = 128
NPAGES = 2
PAST = PAGE * NPAGES
L = PAST + 1
HD = 64
NH = 8
NI = 4
FF = 4 * D
P = 128
KD = D // P
TOK = SEQ + NB
HALVES = (slice(0, SEQ // 2), slice(SEQ // 2, TOK))
WIDE = TOK - SEQ // 2
NT = SEQ // P
TILES = NT + 1
TOPK_P = min(256, SEQ // 4)
TOPK_S = min(256, L // 4)
W = 512
W_IDX = NI * HD + HD + NI
UNIT = 2048
SLOTS = 4
U_PROJ, U_OUT, U_UP = 16, 4, 8
UNITS = U_PROJ + U_OUT + 4 * U_UP
CHUNKS = 8
CONSTS = 13
FT = 16
ATT_FROM = 4 * TILES + 3
ATT_STEPS = NT * NH + 3
CSLOTS = 3
EPS = 1e-6
NEG = -1e30
MARK = -3e38
ATT_SCALE = HD ** -0.5


def rows(t):
    return P if t < NT else NB


def token_cols(t):
    return slice(t * P, t * P + rows(t))


def span(h):
    return HALVES[h].stop - HALVES[h].start


def tile_order(c):
    return [NT] + list(range(NT)) if c == CHUNKS - 1 else list(range(TILES))


def head_steps(c, i):
    def done(n, k):
        tiles = range(ATT_FROM, 7 * TILES)
        cost = [KD * (2 if m % TILES < NT else 1) for m in tiles]
        here = sum(cost[0:n - ATT_FROM]) + k * cost[n - ATT_FROM] // KD
        return here * ATT_STEPS // sum(cost)

    n = c * TILES + i
    return [(k, done(n, k)) for k in range(KD) if done(n, k + 1) > done(n, k)]


def product_items():
    both = [(m, h) for m in range(2 * FT) for h in range(2)]
    out = [("out", m, h, U_PROJ + m // 2) for h in range(2) for m in range(KD)]
    u = U_PROJ + U_OUT
    for half in range(2):
        first = [(m, h) for h in range(2) for m in range(4)] if half == 0 else both[0:8]
        out += [(f"up{half}", m, h, u + m // 2) for m, h in first + both[8:2 * FT]]
        u += U_UP
        last = [(m, h) for h in range(2) for m in range(4, KD)] if half == 1 else both[8:2 * KD]
        out += [(f"down{half}", m, h, u + m) for m, h in both[0:8] + last]
        u += KD
    return out


def square_order():
    out = [(2, 0, k) for k in range(KD)]
    for m in range(KD):
        out += [(2, 1, m)] + ([(3, 0, 2 * m - 2), (3, 0, 2 * m - 1)] if 1 <= m <= 4 else [])
    out += [(3, 1, k) for k in range(KD)]
    out += [(4, h, m) for m in range(4) for h in range(2)] + [(4, 0, m) for m in range(4, KD)]
    out += [(4, 1, 4)] + [(5, 0, k) for k in range(4)] + [(4, 1, 5)] + [(5, 0, k) for k in range(4, KD)]
    return out + [(4, 1, 6), (4, 1, 7)] + [(5, 1, k) for k in range(KD)]


ITEMS = product_items()
SQUARES = square_order()


def items_of(kind):
    return [n for n, it in enumerate(ITEMS) if it[0] == kind]


def item_bank(n):
    return n % 2 if n < KD else n % 4


def square_number(norm, h, k):
    n = SQUARES.index((norm, h, k)) + 1
    return n, sum(1 for s in SQUARES[0:n] if s[2] > 0)


def counter():
    n = {}

    def up(sem):
        n[sem.num] = n.get(sem.num, 0) + 1
        return n[sem.num]

    return n, up


def build(nc, x, w_idx, w_all, gains, g_first, g_ret, cache_k, cache_v, cache_ki, state, pages, tab_cos, tab_sin,
          dmask, k_decay, q_decay, c_decay, s_gamma, ident, expand, select, diag, causal, sum_parts,
          y, k_out, v_out, ki_out, ret_out, ks_out, vs_out, kis_out, rets_out):
    ctx = ExitStack()
    with ctx:
        def sb(name, shape, dt=F32):
            return ctx.enter_context(nc.sbuf_tensor(name, shape, dt))

        x_feat = sb("x_feat", [P, KD, TOK])
        h_feat = sb("h_feat", [P, KD, TOK])
        mix = sb("mix", [P, KD, TOK])
        wring = [sb(f"wring{i}", [P, UNIT]) for i in range(SLOTS)]
        big = sb("big", [P, 4 * TILES * W + 3 * 4 * SEQ])
        osb = big[:, 0:KD * TOK].rearrange("p (j n) -> p j n", n=TOK)
        ff = big[:, KD * TOK:(FT + KD) * TOK].rearrange("p (j n) -> p j n", n=TOK)
        at = [0]

        def part(size, **kw):
            at[0] += size
            return big[:, at[0] - size:at[0]].rearrange("p (t n) -> p t n", **kw)

        kT = part(4 * SEQ, n=SEQ)
        zr = [part(TILES * W, n=W) for _ in range(2)]
        v_tok = part(TILES * W, n=W)
        gate = part(TILES * W, n=W)
        qT = part(4 * SEQ, n=SEQ)
        kbd = part(NT * W, n=W)
        qz = [sb(f"qz{i}", [P, NH, P]) for i in range(2)]
        qiT = kbd[:, 0:2, :]
        kiz = [qz[0][:, j:NH:2, :] for j in range(2)]
        wi = sb("wi", [P, TILES, NI])
        bias = sb("bias", [P, 128 + 256 + 384 + 512])
        b_at = [0, 128, 384, 768]
        top8 = sb("top8", [P, 8])
        s_sbw = [sb(f"s_sb{i}", [P, TOK]) for i in range(2)]
        s_sb = [a[:, 0:W] for a in s_sbw]
        p_sbw = [sb(f"p_sb{i}", [P, TOK]) for i in range(2)]
        p_sb = [a[:, 0:W] for a in p_sbw]
        pt_sbw = [sb("pt_sb0", [P, TOK]), sb("pt_sb1", [P, 2 * WIDE])]
        pt_sb = [a[:, 0:W] for a in pt_sbw]
        temps = sb("temps", [P, 3 * W])
        sqr = [pt_sbw[1][:, i * WIDE:(i + 1) * WIDE] for i in range(2)]
        attm = temps[:, 0:NH * P].rearrange("p (h n) -> p h n", n=P)
        qTd = temps[:, NH * P:NH * P + 4 * P].rearrange("p (h n) -> p h n", n=P)
        raw = [temps[:, i * W:(i + 1) * W] for i in range(3)]
        rt = p_sb
        s_bd = sb("s_bd", [P, 4, P])
        s_tmp = s_sb[0][:, 0:4 * HD].rearrange("p (h d) -> p h d", d=HD)
        mx = sb("mx", [P, 2]); neg_mx = sb("neg_mx", [P, 2])
        rsum = sb("rsum", [P, 2]); rinv = sb("rinv", [P, 2])
        gn_mu = sb("gn_mu", [P, TILES, NH]); gn_var = sb("gn_var", [P, TILES, NH])
        ssum, std, upd = pt_sbw[0], s_sbw[0], s_sbw[1]
        rstd_post, rstd_ffn = p_sbw[0], sb("rstd_ffn", [P, TOK])
        rope_tmp = osq = rstd_ffn[:, 0:W]
        std_tok = sb("std_tok", [P, TILES])
        rtok = sb("rtok", [P, 3, TILES])
        gate_flat = gate.rearrange("p t n -> p (t n)")
        kit = gate_flat[0:HD, 0:NB * L].rearrange("p (b k) -> p b k", k=L)
        qis = sb("qis", [HD, NB, 32])
        wx = sb("wx", [NB, 2, P]); wm = sb("wm", [P, 2, NB])
        rs = sb("rs", [P, 2, L]); works = sb("works", [NB, L]); bias_s = sb("bias_s", [NB, L])
        tops = sb("tops", [NB, 8])
        qs = sb("qs", [P, NB, P]); kTs = sb("kTs", [P, 4, NB])
        caches = sb("caches", [P, CSLOTS * 4 * L])
        cring = [caches[:, i * 4 * L:(i + 1) * 4 * L] for i in range(CSLOTS)]
        st = caches[:, 0:2048]
        ps_s = rs
        mxs = sb("mxs", [P, 2]); nms = sb("nms", [P, 2]); sms = sb("sms", [P, 2]); ris = sb("ris", [P, 2])
        vrep = gate[:, 0:2, :]
        pts = gate[:, 2, :].rearrange("p (i n) -> p i n", n=P)
        qr = sb("qr", [P, 32]); kr = sb("kr", [P, 32]); vr = sb("vr", [P, HD])
        op = sb("op", [P, HD]); op2 = caches[0:NB, 2048:3072].rearrange("p (h j e) -> p h j e", h=NH, j=2); o_s = s_sb[1][0:NB]
        gcol = sb("gcol", [P, 4, KD]); gfirst = sb("gfirst", [P, KD]); gret = sb("gret", [P, W])
        cosT = sb("cosT", [P, TILES, HD]); sinT = sb("sinT", [P, TILES, HD])
        dm = sb("dm", [P, NH, P]); kdec = sb("kdec", [P, NH]); qdec = sb("qdec", [P, 4, P])
        cdec = sb("cdec", [P, 4]); gam = sb("gam", [P, 1])
        idn = sb("idn", [P, P]); exps = sb("exps", [NB, 2, P]); sel = sb("sel", [P, 2, NB])
        parts = sb("parts", [P, W]); addp = sb("addp", [P, NB]); dg = sb("dg", [P, NH]); ones = sb("ones", [P, P]); eps = sb("eps", [P, 1])
        pg = sb("pg", [1, NB * NPAGES], I32)
        ps = ctx.enter_context(nc.psum_tensor("ps", [P, 8, 512], F32))

        def sem(name):
            return ctx.enter_context(nc.semaphore(name))

        const_in = sem("const_in"); zeroed = sem("zeroed"); layer_go = sem("layer_go"); y_out = sem("y_out")
        x_in = [sem(f"x_in{i}") for i in range(KD // 2)]
        gfirst_in = sem("gfirst_in")
        first_w = sem("first_w")
        pages_in = sem("pages_in")
        first_sq = sem("first_sq")
        first_sum = sem("first_sum")
        first_h = sem("first_h")
        gains_in = sem("gains_in")
        next_w = sem("next_w")
        kidx_in = sem("kidx_in")
        state_in = sem("state_in")
        sq_ready = sem("sq_ready")
        sq_used = sem("sq_used")
        stat_mm = sem("stat_mm")
        std_ready = sem("std_ready")
        rstd_ready = sem("rstd_ready")
        tok_mm = sem("tok_mm")
        tok_std = sem("tok_std")
        rtok_ready = sem("rtok_ready")
        h_ready = sem("h_ready")
        proj_done = sem("proj_done")
        part_mm = sem("part_mm")
        part_read = sem("part_read")
        proj_read = sem("proj_read")
        rope_done = sem("rope_done")
        tr_mm = sem("tr_mm")
        tr_read = sem("tr_read")
        ts_mm = sem("ts_mm")
        ts_read = sem("ts_read")
        dot_mm = sem("dot_mm")
        dot_read = sem("dot_read")
        comb_done = sem("comb_done")
        sdot_mm = sem("sdot_mm")
        srelu_done = sem("srelu_done")
        wx_ready = sem("wx_ready")
        wm_mm = sem("wm_mm")
        wm_ready = sem("wm_ready")
        ssc_mm = sem("ssc_mm")
        ssc_read = sem("ssc_read")
        sbias_ready = sem("sbias_ready")
        bias_ready = sem("bias_ready")
        knew_done = sem("knew_done")
        cache_used = sem("cache_used")
        smx_ready = sem("smx_ready")
        sp_exp = sem("sp_exp")
        sp_ready = sem("sp_ready")
        spt_mm = sem("spt_mm")
        spt_ready = sem("spt_ready")
        vrep_mm = sem("vrep_mm")
        vrep_ready = sem("vrep_ready")
        om_ready = sem("om_ready")
        as_mm = sem("as_mm")
        as_read = sem("as_read")
        qz_ready = sem("qz_ready")
        att_mm = sem("att_mm")
        att_read = sem("att_read")
        p_exp = sem("p_exp")
        p_ready = sem("p_ready")
        pt_mm = sem("pt_mm")
        pt_ready = sem("pt_ready")
        pv_mm = sem("pv_mm")
        blk_read = sem("blk_read")
        gate_exp = sem("gate_exp")
        gain_ready = sem("gain_ready")
        gate_ready = sem("gate_ready")
        ra_mm = sem("ra_mm")
        attm_ready = sem("attm_ready")
        qtd_ready = sem("qtd_ready")
        su_mm = sem("su_mm")
        sbd_ready = sem("sbd_ready")
        o_mm = sem("o_mm")
        o_read = sem("o_read")
        osq_ready = sem("osq_ready")
        kbd_ready = sem("kbd_ready")
        bounce = sem("bounce")
        bounce_o = sem("bounce_o")
        sret_ready = sem("sret_ready")
        gvar_ready = sem("gvar_ready")
        gstd_ready = sem("gstd_ready")
        b_ready = sem("b_ready")
        bt_mm = sem("bt_mm")
        bt_read = sem("bt_read")
        mt_done = sem("mt_done")
        wo_read = sem("wo_read")
        up_read = sem("up_read")
        dn0_read = sem("dn0_read")
        dn1_read = sem("dn1_read")
        f_ready = sem("f_ready")
        x_ready = sem("x_ready")
        out_ki = sem("out_ki")
        out_k = sem("out_k")
        out_v = sem("out_v")
        out_r = sem("out_r")
        sopart = sem("sopart")
        ended = sem("ended")
        act_step = sem("act_step")
        dve_step = sem("dve_step")
        pool_step = sem("pool_step")
        w_slot = [sem(f"w_slot{i}") for i in range(SLOTS)]
        c_slot = [sem(f"c_slot{i}") for i in range(CSLOTS)]
        cleared = range(gains_in.num, c_slot[-1].num + 1)

        block = ctx.enter_context(nc.Block())

        def next_layer(eng, l):
            eng.drain().then_inc(ended, 1)
            eng.wait_ge(layer_go, l + 1)

        def unit_used(u):
            if u < U_PROJ:
                return proj_done, TILES * (u // 2 + 1)
            return mt_done, max(n for n, it in enumerate(ITEMS) if it[3] == u) + 1

        def item_free(n):
            before = [m for m in range(n) if item_bank(m) == item_bank(n)]
            if not before:
                return None
            kind = ITEMS[before[-1]][0]
            read = {"out": wo_read, "up0": up_read, "up1": up_read, "down0": dn0_read, "down1": dn1_read}[kind]
            return read, items_of(kind).index(before[-1]) + 1 + (2 * FT if kind == "up1" else 0)

        @block.sync
        def _(sp):
            sp.dma_start(pg[:], pages).then_inc(pages_in, 16)
            for k in range(0, KD, 2):
                sp.dma_start(x_feat[:, k:k + 2, :], x[:, k:k + 2, :]).then_inc(x_in[k // 2], 16)
            for u in range(2):
                sp.dma_start(wring[u][:, 0:4 * W_IDX], w_idx[0, u]).then_inc(first_w, 16)
            with sp.Fori(0, DEPTH) as l:
                def layer(a, pat):
                    return a[bass.ds(l, 1)].rearrange(pat)

                def unit(u):
                    if u >= SLOTS:
                        sm, v = unit_used(u - SLOTS)
                        sp.wait_ge(sm, v)
                    src = w_all[bass.ds(l, 1), u - 2:u - 1].rearrange("a b p n -> (a b p) n")
                    sp.dma_start(wring[u % SLOTS][:], src).then_inc(w_slot[u % SLOTS], 16)

                def cache_tile(i):
                    if i >= CSLOTS:
                        sp.wait_ge(cache_used, i - CSLOTS + 1)
                    c, b = cring[i % CSLOTS], i % NB
                    for j in range(NPAGES):
                        pid = page[b * NPAGES + j]
                        if i < NB:
                            src = cache_k[bass.ds(l, 1), bass.ds(pid, 1)].rearrange("a b (h p) k -> p (a b h) k", p=P)
                            dst = c[:].rearrange("p (h k) -> p h k", k=L)[:, :, j * PAGE:(j + 1) * PAGE]
                        else:
                            src = cache_v[bass.ds(l, 1), bass.ds(pid, 1)].rearrange("a b k n -> (a b k) n")
                            dst = c[:, j * W:(j + 1) * W]
                        sp.dma_start(dst, src).then_inc(c_slot[i % CSLOTS], 16)

                for u in range(2, 4):
                    unit(u)
                sp.wait_ge(pages_in, 16)
                page = [sp.value_load(pg[0:1, i:i + 1], min_val=0, max_val=cache_k.shape[1] - 1)
                        for i in range(NB * NPAGES)]
                sp.dma_start(gcol[:], layer(gains, "a p k n -> (a p) k n")).then_inc(gains_in, 16)
                sp.dma_start(gret[:], g_ret[bass.ds(l, 1)].to_broadcast([P, W])).then_inc(gains_in, 16)
                for b in range(NB):
                    for j in range(NPAGES):
                        src = cache_ki[bass.ds(l, 1), bass.ds(page[b * NPAGES + j], 1)].rearrange("a b d k -> (a b d) k")
                        sp.dma_start(kit[:, b, j * PAGE:(j + 1) * PAGE], src).then_inc(kidx_in, 16)
                for u in range(4, 8):
                    unit(u)
                for i in range(CSLOTS):
                    cache_tile(i)
                for u in range(8, 10):
                    unit(u)
                for i in range(CSLOTS, NB + CSLOTS):
                    cache_tile(i)
                for u in range(10, 12):
                    unit(u)
                for i in range(NB + CSLOTS, 2 * NB):
                    cache_tile(i)
                sp.wait_ge(cache_used, 2 * NB)
                sp.dma_start(st, layer(state, "a p n -> (a p) n")).then_inc(state_in, 16)
                for u in range(12, UNITS):
                    unit(u)
                for u in range(2):
                    sp.wait_ge(mt_done, unit_used(UNITS - SLOTS + u)[1])
                    src = w_idx[bass.ds(l + 1, 1), u:u + 1].rearrange("a b p n -> (a b p) n")
                    sp.dma_start(wring[u][:, 0:4 * W_IDX], src).then_inc(next_w, 16)
                sp.wait_ge(next_w, 32)
                sp.drain().then_inc(ended, 1)
                sp.wait_ge(ended, 5)
                sp.sem_clear(cleared)
                sp.sem_inc(layer_go, 1)
            sp.dma_start(y, x_feat[:]).then_inc(y_out, 16)
            sp.wait_ge(y_out, 16)

        @block.tensor
        def _(pe):
            mm = nc.tensor.matmul
            pe.wait_ge(zeroed, 1)
            pe.wait_ge(first_h, KD)
            pe.wait_ge(first_w, 32)
            counts, up = counter()

            def unit_here(u):
                if u >= 2:
                    pe.wait_ge(w_slot[u % SLOTS], 16 * (u // SLOTS + (u % SLOTS >= 2)))

            def stats(norm, h):
                pe.wait_ge(sq_used, square_number(norm, h, KD - 1)[1])
                if counts.get(stat_mm.num, 0):
                    pe.wait_ge(std_ready, counts[stat_mm.num])
                mm(ps[:, 4, 0:span(h)], ones[:], ssum[:, HALVES[h]], start=True, stop=True).then_inc(stat_mm, 1)
                up(stat_mm)

            def add_parts(n):
                c = n // TILES
                pe.wait_ge(part_read, c + 1)
                width = W if c else W_IDX
                mm(ps[0:NB, n % 2, 0:width], addp[:], parts[:, 0:width], start=True, stop=True).then_inc(proj_done, 1)

            def project(c, between):
                width = W if c else W_IDX
                for i, t in enumerate(tile_order(c)):
                    n = c * TILES + i
                    if i == 0:
                        unit_here(2 * c)
                    if n >= 2:
                        pe.wait_ge(proj_read, n - 1)
                    ks = range(KD) if t < NT else (0, 2, 4, 6, 1, 3, 5, 7)
                    for j, k in enumerate(ks):
                        if i == 0 and j == (4 if t < NT else 2):
                            unit_here(2 * c + 1)
                        wt = wring[(2 * c + k // 4) % SLOTS][:, (k % 4) * width:(k % 4 + 1) * width]
                        if t < NT:
                            last = mm(ps[:, n % 2, 0:width], h_feat[:, k, token_cols(t)], wt,
                                      start=(k == 0), stop=(k == KD - 1))
                        else:
                            q4 = 32 * (k // 2)
                            last = mm(ps[q4:q4 + 32, n % 2, 0:width], h_feat[:, k, TOK - 32:TOK], wt,
                                      start=(k % 2 == 0), stop=(k % 2 == 1))
                        if j == 1 and n and (i == 0 or tile_order(c)[i - 1] == NT):
                            add_parts(n - 1)
                        if j < KD - 1:
                            between(i, j)
                    last.then_inc(proj_done if t < NT else part_mm, 1)
                    between(i, KD - 1)

            def transpose_group(z, c0, c1):
                g = counts.get(tr_mm.num, 0)
                if g >= 2:
                    pe.wait_ge(tr_read, g - 1)
                for t in range(NT):
                    last = nc.tensor.transpose(ps[0:c1 - c0, 4 + g % 2, t * P:(t + 1) * P], z[:, t, c0:c1], idn[:])
                last.then_inc(tr_mm, 1)
                up(tr_mm)

            def transpose_sample(z, cols):
                for i, (c0, c1) in enumerate(cols):
                    last = nc.tensor.transpose(ps[0:c1 - c0, 7, i * NB:(i + 1) * NB], z[0:NB, NT, c0:c1], idn[0:NB, 0:NB])
                last.then_inc(ts_mm, 1)

            pairs = [(i * P, (i + 1) * P) for i in range(4)]
            heads = [(i * HD, (i + 1) * HD) for i in range(NI + 1)]

            def beside_idx(i, k):
                if (i, k) == (1, 0):
                    pe.wait_ge(const_in, 16 * CONSTS)
                if (i, k) == (0, KD - 1):
                    pe.wait_ge(first_sum, KD - 1)
                    for t in range(TILES):
                        last = mm(ps[0:rows(t), 6, t:t + 1], ssum[:, token_cols(t)], ones[:, 0:1], start=True, stop=True)
                    last.then_inc(tok_mm, 1)

            def beside_q(i, k):
                if (i, k) == (0, KD - 1):
                    pe.wait_ge(rope_done, TILES)
                    for c0, c1 in [(0, P), (P, 2 * P), (2 * P, 2 * P + HD)]:
                        transpose_group(zr[0], c0, c1)
                    transpose_sample(zr[0], heads)
                if 1 <= i <= 3 and k % 2:
                    j = 4 * (i - 1) + k // 2
                    b, h = 1 + j // NI, j % NI
                    if j == 0:
                        pe.wait_ge(tr_read, 3)
                    if j >= 2:
                        pe.wait_ge(dot_read, j - 1)
                    mm(ps[:, 4 + j % 2, 0:(b + 1) * P], qiT[:, h // 2, b * P:(b + 1) * P], kiz[h % 2][:, 0:b + 1, :],
                       start=True, stop=True).then_inc(dot_mm, 1)
                if (i, k) == (3, KD - 1):
                    pe.wait_ge(kidx_in, 16 * NB * NPAGES)
                    pe.wait_ge(ts_read, 1)
                    for b in range(NB):
                        last = mm(ps[32 * (b % 4):32 * (b % 4) + 32, 2 + b // 4, 0:L], qis[:, b, :], kit[:, b, :],
                                  start=True, stop=True)
                    last.then_inc(sdot_mm, 1)

            def beside_k(i, k):
                if (i, k) == (0, 3):
                    pe.wait_ge(wx_ready, 1)
                    for g in range(2):
                        last = nc.tensor.transpose(ps[:, 6, 64 + g * NB:64 + (g + 1) * NB], wx[:, g, :], idn[0:NB, 0:NB])
                    last.then_inc(wm_mm, 1)
                if (i, k) == (0, KD - 1):
                    pe.wait_ge(wm_ready, 1)
                    pe.wait_ge(srelu_done, 1)
                    for g in range(2):
                        last = mm(ps[0:NB, 6, P:P + L], wm[:, g, :], rs[:, g, :], start=(g == 0), stop=(g == 1))
                    last.then_inc(ssc_mm, 1)
                if (i, k) == (1, KD - 1):
                    pe.wait_ge(rope_done, 2 * TILES)
                    pe.wait_ge(dot_read, 3 * NI)
                    for c0, c1 in pairs:
                        transpose_group(zr[1], c0, c1)
                    transpose_sample(zr[1], pairs)

            def beside_v(i, k):
                if (i, k) == (1, KD - 1):
                    pe.wait_ge(rope_done, 3 * TILES)
                    pe.wait_ge(ts_read, 2)
                    for c0, c1 in pairs:
                        transpose_group(zr[0], c0, c1)
                    transpose_sample(zr[0], pairs)
                if 2 <= i <= 3 and k % 2:
                    b = 4 * (i - 2) + k // 2
                    g, q4 = b // 4, 32 * (b % 4)
                    if b == 0:
                        pe.wait_ge(sbias_ready, 1)
                    if b % 4 == 0:
                        mm(ps[:, 2 + g, 0:L], exps[:, g, :], bias_s[:], start=True, stop=False, skip_group_check=True)
                    pe.wait_ge(c_slot[b % CSLOTS], 16 * NPAGES * (b // CSLOTS + 1))
                    pe.wait_ge(knew_done, b + 1)
                    kc = cring[b % CSLOTS][:].rearrange("p (h k) -> p h k", k=L)
                    for h in range(4):
                        last = mm(ps[q4:q4 + 32, 2 + g, 0:L], qs[:, b, 32 * h:32 * h + 32], kc[:, h, :],
                                  start=False, stop=(h == 3), skip_group_check=True)
                    last.then_inc(cache_used, 1)

            def attend(i):
                if 2 <= i < NT * NH + 2:
                    j = i - 2
                    pe.wait_ge(p_ready, j + 1)
                    if j >= 2:
                        pe.wait_ge(pt_ready, j - 1)
                    else:
                        pe.wait_ge(om_ready, 2)
                    for m in range(j // NH + 1):
                        last = nc.tensor.transpose(ps[:, 2 + j % 2, m * P:(m + 1) * P], p_sb[j % 2][:, m * P:(m + 1) * P], idn[:])
                    last.then_inc(pt_mm, 1)
                if i < NT * NH:
                    b, h = divmod(i, NH)
                    if h == 0:
                        pe.wait_ge(qz_ready, b + 1)
                    if i == 0:
                        pe.wait_ge(tr_read, 11)
                    if i >= 2:
                        pe.wait_ge(att_read, i - 1)
                    mm(ps[:, 4 + i % 2, 0:(b + 1) * P], qz[b % 2][:, h, :], kT[:, h // 2, 0:(b + 1) * P],
                       start=True, stop=True).then_inc(att_mm, 1)
                if i >= 3:
                    j = i - 3
                    b, h = divmod(j, NH)
                    pe.wait_ge(pt_ready, j + 1)
                    if h == 0 and b >= 2:
                        pe.wait_ge(blk_read, b - 1)
                    if h == 0 and b == 1:
                        pe.wait_ge(as_read, 1)
                    r = HD * (h % 2)
                    for m in range(b + 1):
                        last = mm(ps[r:r + HD, 6 + b % 2, (h // 2) * P:(h // 2 + 1) * P],
                                  v_tok[:, m, h * HD:(h + 1) * HD], pt_sb[j % 2][:, m * P:(m + 1) * P],
                                  start=(m == 0), stop=(m == b))
                    last.then_inc(pv_mm, 1)

            def beside_heads(c, i, k):
                for slot, step in head_steps(c, i):
                    if slot == k:
                        attend(step)

            def beside_qb(i, k):
                if (i, k) == (0, 3):
                    pe.wait_ge(ssc_read, 1)
                    pe.wait_ge(ts_read, 3)
                    pe.wait_ge(proj_read, 4 * TILES)
                    for g in range(2):
                        last = mm(ps[:, 6 + g, 0:W], exps[:, g, :], v_tok[0:NB, NT, :], start=True, stop=True)
                    last.then_inc(vrep_mm, 1)
                if (i, k) == (0, KD - 1):
                    pe.wait_ge(sp_ready, 2)
                    pe.wait_ge(vrep_ready, 2)
                    for j in range(4):
                        last = nc.tensor.transpose(ps[:, 6, j * P:(j + 1) * P],
                                                   ps_s[:, j // 2, (j % 2) * PAGE:(j % 2 + 1) * PAGE], idn[:])
                    last.then_inc(spt_mm, 1)
                if 1 <= i <= 2 and k % 2:
                    b = 4 * (i - 1) + k // 2
                    if b == 0:
                        pe.wait_ge(spt_ready, 1)
                    g, q4, m = b // 4, 32 * (b % 4), NB + b
                    pe.wait_ge(c_slot[m % CSLOTS], 16 * NPAGES * (m // CSLOTS + 1))
                    for j in range(NPAGES):
                        last = mm(ps[q4:q4 + 32, 2 + g, 0:W], pts[:, 2 * g + j, q4:q4 + 32],
                                  cring[m % CSLOTS][:, j * W:(j + 1) * W], start=(j == 0), stop=(j == 1))
                    last.then_inc(cache_used, 1)
                if i >= 3:
                    beside_heads(4, i, k)

            def beside_kb(i, k):
                beside_heads(5, i, k)
                if (i, k) == (0, KD - 1):
                    pe.wait_ge(om_ready, 2)
                    for h in range(4):
                        for g in range(2):
                            last = mm(ps[:, 7, h * NB:(h + 1) * NB], vrep[:, g, h * P:(h + 1) * P], sel[:, g, :],
                                      start=(g == 0), stop=(g == 1))
                    last.then_inc(as_mm, 1)

            def chunk_scores(c):
                pe.wait_ge(qz_ready, NT + c + 1)
                for g in range(2):
                    if c:
                        pe.wait_ge(attm_ready, 2 * (c - 1) + g + 1)
                    for h in range(4 * g, 4 * g + 4):
                        last = mm(ps[:, 4 + g, (h % 4) * P:(h % 4 + 1) * P], kT[:, h // 2, c * P:(c + 1) * P],
                                  qz[c % 2][:, h, :], start=True, stop=True)
                    last.then_inc(ra_mm, 1)

            def chunk_state(c):
                pe.wait_ge(proj_read, 7 * TILES + c + 2)
                if c == 0:
                    pe.wait_ge(kbd_ready, NT)
                    pe.wait_ge(pt_ready, NT * NH)
                else:
                    pe.wait_ge(sbd_ready, c)
                for h in range(4):
                    last = mm(ps[:, 2, h * P:(h + 1) * P], kbd[:, c, h * P:(h + 1) * P],
                              v_tok[:, c, h * P:(h + 1) * P], start=True, stop=True)
                last.then_inc(su_mm, 1)

            def chunk_output(c):
                pe.wait_ge(attm_ready, 2 * c + 2)
                if c == 0:
                    pe.wait_ge(blk_read, NT)
                if c >= 2:
                    pe.wait_ge(o_read, c - 1)
                if c:
                    pe.wait_ge(qtd_ready, c)
                for h in range(4):
                    if c:
                        mm(ps[:, 6 + c % 2, h * P:(h + 1) * P], qTd[:, h, :], s_bd[:, h, :], start=True, stop=False)
                    for e in (2 * h, 2 * h + 1):
                        last = mm(ps[:, 6 + c % 2, e * HD:(e + 1) * HD], attm[:, e, :], v_tok[:, c, e * HD:(e + 1) * HD],
                                  start=(c == 0), stop=(c == 0 or e % 2 == 1))
                last.then_inc(o_mm, 1)

            def chunk_turn(t):
                pe.wait_ge(b_ready, t + 1)
                if t:
                    pe.wait_ge(bt_read, t)
                r = rows(t)
                for h in range(4):
                    last = nc.tensor.transpose(ps[:, 3, h * r:(h + 1) * r], zr[1][0:r, t, h * P:(h + 1) * P], idn[0:r, 0:r])
                last.then_inc(bt_mm, 1)

            def beside_vb(i, k):
                if i == 0 and k % 2:
                    if k == 1:
                        pe.wait_ge(rope_done, 5 * TILES)
                        pe.wait_ge(att_read, NT * NH)
                    transpose_group(zr[1], *pairs[k // 2])
                if i == 1 and k < 4:
                    transpose_group(zr[0], *pairs[k])
                if (i, k) == (1, 5):
                    pe.wait_ge(tr_read, 19)
                    chunk_scores(0)
                if i >= 2:
                    if k == 1:
                        chunk_state(i - 2)
                    if k == 4:
                        chunk_output(i - 2)
                    if k == 5 and i >= 3:
                        chunk_turn(i - 3)
                    if k == 7:
                        chunk_scores(i - 1)

            def item(n):
                kind, m, h, u = ITEMS[n]
                free = item_free(n)
                if free:
                    pe.wait_ge(free[0], free[1])
                unit_here(u)
                nk = KD if kind[0] in "ou" else FT
                src = mix if kind == "out" else h_feat if kind[0] == "u" else ff
                off = 0 if nk == FT else (m % 2) * KD
                for k in range(nk):
                    if kind == "up0" and m == 0:
                        pe.wait_ge(h_ready, KD * h + k + 1)
                    if nk == FT and m == 0 and h == 0:
                        half = int(kind[-1])
                        pe.wait_ge(f_ready, 2 * FT * half + 1 + max(items_of(f"up{half}").index(ITEMS.index(it)) for it in ITEMS
                                                                   if it[0] == f"up{half}" and it[1] == k))
                    last = mm(ps[:, item_bank(n), 0:span(h)], wring[u % SLOTS][:, (off + k) * P:(off + k + 1) * P],
                              src[:, k, HALVES[h]], start=(k == 0), stop=(k == nk - 1))
                    if n == 2 * KD and k == 5:
                        stats(2, 1)
                last.then_inc(mt_done, 1)

            with pe.Fori(0, DEPTH) as l:
                counts.clear()
                project(0, beside_idx)
                project(1, beside_q)
                project(2, beside_k)
                project(3, beside_v)
                project(4, beside_qb)
                project(5, beside_kb)
                project(6, lambda i, k: beside_heads(6, i, k))
                project(7, beside_vb)
                for n in range(len(ITEMS)):
                    if n == 0:
                        pe.wait_ge(as_read, 1)
                        pe.wait_ge(bt_read, 2)
                        pe.wait_ge(proj_read, 8 * TILES)
                    if n == KD:
                        pe.wait_ge(bt_read, TILES)
                        pe.wait_ge(sbd_ready, NT)
                    item(n)
                    if n == 0:
                        chunk_state(3)
                        chunk_output(3)
                    if n == 1:
                        chunk_turn(2)
                    if n == 4:
                        chunk_turn(3)
                    if n == 5:
                        chunk_turn(4)
                    if n == KD:
                        stats(2, 0)
                    if n == KD + 5:
                        stats(3, 0)
                    if n == 2 * KD + 4:
                        stats(3, 1)
                    if n == len(ITEMS) - 4:
                        stats(4, 0)
                stats(4, 1)
                next_layer(pe, l)

        @block.scalar
        def _(act):
            act.dma_start(gfirst[:], g_first).then_inc(gfirst_in, 16)
            counts, up = counter()
            first = [ssum, pt_sbw[1][:, 0:TOK], p_sbw[1]]
            act.wait_ge(gfirst_in, 16)
            for k in range(KD):
                act.wait_ge(x_in[k // 2], 16)
                nc.scalar.activation(h_feat[:, k, :], x_feat[:, k, :], ACT.Copy, scale=gfirst[:, k:k + 1]).then_inc(first_h, 1)
                if k >= 3:
                    act.wait_ge(first_sum, k - 2)
                nc.scalar.activation(first[0 if k == 0 else 1 + k % 2][:], x_feat[:, k, :], ACT.Square).then_inc(first_sq, 1)
            loads = [(idn[:], ident), (cosT[:], tab_cos), (sinT[:], tab_sin), (exps[:], expand),
                     (bias[:, 0:P], causal), (sel[:], select), (dg[:], diag), (dm[:], dmask), (kdec[:], k_decay),
                     (qdec[:], q_decay), (cdec[:], c_decay), (gam[:], s_gamma), (addp[:], sum_parts)]
            assert len(loads) == CONSTS
            for dst, src in loads:
                act.dma_start(dst, src).then_inc(const_in, 16)
            act.wait_ge(zeroed, 1)
            act.wait_ge(const_in, 16 * CONSTS)
            act.wait_ge(first_h, KD)

            def square(norm, h, k, src):
                number, added = square_number(norm, h, k)
                if k == 0:
                    if norm > 2:
                        act.wait_ge(stat_mm, {(3, 0): 1, (3, 1): 3, (4, 0): 2, (4, 1): 4, (5, 0): 5, (5, 1): 6}[norm, h])
                    dst = ssum[:, HALVES[h]]
                else:
                    if added >= 3:
                        act.wait_ge(sq_used, added - 2)
                    dst = sqr[added % 2][:, 0:span(h)]
                nc.scalar.activation(dst, src, ACT.Square).then_inc(sq_ready, 1)
                act.wait_ge(sq_ready, up(sq_ready))

            def deviation(h):
                n = counts.get(std_ready.num, 0)
                act.wait_ge(stat_mm, n + 1)
                if n:
                    act.wait_ge(rstd_ready, n)
                nc.scalar.activation(std[:, HALVES[h]], ps[:, 4, 0:span(h)], ACT.Sqrt, bias=eps[:]).then_inc(std_ready, 1)
                act.wait_ge(std_ready, up(std_ready))

            def normed(norm, h, k, n):
                act.wait_ge(x_ready, n)
                nc.scalar.activation(h_feat[:, k, HALVES[h]], x_feat[:, k, HALVES[h]], ACT.Copy,
                                     scale=gcol[:, 1 if norm == 3 else 3, k:k + 1]).then_inc(h_ready, 1)
                square(norm, h, k, x_feat[:, k, HALVES[h]])

            def take_parts(c):
                n, width = c * TILES + tile_order(c).index(NT), W if c else W_IDX
                act.wait_ge(part_mm, c + 1)
                nc.scalar.activation(parts[:, 0:width], ps[:, n % 2, 0:width], ACT.Copy).then_inc(part_read, 1)
                act.wait_ge(part_read, up(part_read))

            def evacuate(c, i):
                t = tile_order(c)[i]
                n, r = c * TILES + i, rows(t)
                if t == NT and counts.get(part_read.num, 0) == c:
                    take_parts(c)
                act.wait_ge(proj_done, n + 1)
                src = ps[0:r, n % 2, 0:W if c else W_IDX]
                if c in (3, 7):
                    dst, sc = v_tok[0:r, t, :], 0
                elif c == 6:
                    dst, sc = gate[0:r, t, :], 0
                else:
                    m = {0: 0, 1: 1, 2: 2, 4: 3, 5: 4}[c] * TILES + t
                    if m >= 3:
                        act.wait_ge(rope_done, m - 2)
                    dst, sc = raw[m % 3][0:r, 0:(W if c else W_IDX - NI)], (1 if c == 5 else 0)
                    if c == 0:
                        nc.scalar.activation(wi[0:r, t, :], src[:, W_IDX - NI:W_IDX], ACT.Copy,
                                             scale=rtok[0:r, 2, t:t + 1]).then_inc(act_step, 1)
                        act.wait_ge(act_step, up(act_step))
                        src = src[:, 0:W_IDX - NI]
                nc.scalar.activation(dst, src, ACT.Copy, scale=rtok[0:r, sc, t:t + 1]).then_inc(proj_read, 1)
                act.wait_ge(proj_read, up(proj_read))
                if c == 6:
                    if t >= 3:
                        act.wait_ge(gate_ready, t - 2)
                    elif t == 0:
                        act.wait_ge(rope_done, 5 * TILES)
                    nc.scalar.activation(raw[t % 3][0:r], gate[0:r, t, :], ACT.Exp, scale=-1.0).then_inc(gate_exp, 1)
                    act.wait_ge(gate_exp, up(gate_exp))

            def take_groups(dsts):
                for d in dsts:
                    act.wait_ge(tr_mm, counts.get(tr_read.num, 0) + 1)
                    src = ps[:, 4 + counts.get(tr_read.num, 0) % 2, :]
                    if d is kiz:
                        keys = src[0:HD].rearrange("p (b n) -> p b n", n=P)
                        nc.scalar.activation(kiz[0][0:HD], keys, ACT.Copy).then_inc(act_step, 1)
                        act.wait_ge(act_step, up(act_step))
                        nc.scalar.activation(kiz[1][HD:P], keys, ACT.Copy).then_inc(tr_read, 1)
                        act.wait_ge(tr_read, up(tr_read))
                    else:
                        nc.scalar.activation(d, src, ACT.Copy).then_inc(tr_read, 1)
                        act.wait_ge(tr_read, up(tr_read))

            def attend(i):
                if i >= 11 and (i - 11) % NH == 0:
                    block_out((i - 11) // NH)
                if 2 <= i < NT * NH + 2:
                    j = i - 2
                    act.wait_ge(pt_mm, j + 1)
                    if j >= 2:
                        act.wait_ge(pv_mm, j - 1)
                    n = (j // NH + 1) * P
                    nc.scalar.activation(pt_sb[j % 2][:, 0:n], ps[:, 2 + j % 2, 0:n], ACT.Copy).then_inc(pt_ready, 1)
                    act.wait_ge(pt_ready, up(pt_ready))
                if i < NT * NH:
                    n = (i // NH + 1) * P
                    act.wait_ge(att_read, i + 1)
                    nc.scalar.activation(p_sb[i % 2][:, 0:n], s_sb[i % 2][:, 0:n], ACT.Exp,
                                         bias=neg_mx[:, i % 2:i % 2 + 1], scale=ATT_SCALE,
                                         accum_out=rsum[:, i % 2:i % 2 + 1]).then_inc(p_exp, 1)
                    act.wait_ge(p_exp, up(p_exp))

            def block_out(b):
                act.wait_ge(pv_mm, NH * (b + 1))
                nc.scalar.activation(mix[:, 0:4, b * P:(b + 1) * P], ps[:, 6 + b % 2, :].rearrange("p (h n) -> p h n", h=4),
                                     ACT.Copy).then_inc(blk_read, 1)
                act.wait_ge(blk_read, up(blk_read))

            def gn_root(t):
                act.wait_ge(gvar_ready, t + 1)
                r = rows(t)
                nc.scalar.activation(gn_var[0:r, t, :], gn_var[0:r, t, :], ACT.Sqrt, bias=eps[0:r], scale=1.0 / HD).then_inc(gstd_ready, 1)
                act.wait_ge(gstd_ready, up(gstd_ready))

            def turned(t):
                act.wait_ge(bt_mm, t + 1)
                r = rows(t)
                nc.scalar.activation(mix[:, 4:8, token_cols(t)], ps[:, 3, 0:4 * r].rearrange("p (h n) -> p h n", h=4),
                                     ACT.Copy).then_inc(bt_read, 1)
                act.wait_ge(bt_read, up(bt_read))

            def take_item(n, done):
                kind, m, h, u = ITEMS[n]
                act.wait_ge(mt_done, n + 1)
                nc.scalar.activation(osb[:, m, HALVES[h]], ps[:, item_bank(n), 0:span(h)], ACT.Copy).then_inc(done, 1)
                act.wait_ge(done, up(done))

            with act.Fori(0, DEPTH) as l:
                counts.clear()
                act.wait_ge(tok_mm, 1)
                nc.scalar.activation(std_tok[:, 0:NT], ps[:, 6, 0:NT], ACT.Sqrt, bias=eps[:]).then_inc(tok_std, 1)
                nc.scalar.activation(std_tok[0:NB, NT:TILES], ps[0:NB, 6, NT:TILES], ACT.Sqrt, bias=eps[0:NB]).then_inc(tok_std, 1)
                act.wait_ge(rtok_ready, 1)
                for i in range(TILES):
                    evacuate(0, i)
                evacuate(1, 0)
                take_groups([qiT[:, 0, :], qiT[:, 1, :], kiz])
                act.wait_ge(ts_mm, 1)
                nc.scalar.activation(qis[:, :, 0:NI], ps[0:HD, 7, 0:NI * NB].rearrange("p (h b) -> p b h", b=NB), ACT.Copy).then_inc(act_step, 1)
                act.wait_ge(act_step, up(act_step))
                nc.scalar.activation(kit[:, :, PAST], ps[0:HD, 7, NI * NB:(NI + 1) * NB], ACT.Copy).then_inc(ts_read, 1)
                act.wait_ge(ts_read, up(ts_read))
                act.dma_start(ki_out[bass.ds(l, 1)].rearrange("a (t p) n -> p (a t) n", p=P), zr[0][:, 0:NT, NI * HD:(NI + 1) * HD]).then_inc(out_ki, 16)
                act.dma_start(kis_out[bass.ds(l, 1)].rearrange("a p n -> (a p) n"), zr[0][0:NB, NT, NI * HD:(NI + 1) * HD]).then_inc(out_ki, 16)
                for j in range(3 * NI):
                    b = 1 + j // NI
                    act.wait_ge(dot_mm, j + 1)
                    if j >= 2:
                        act.wait_ge(comb_done, j - 1)
                    nc.scalar.activation(s_sb[j % 2][:, 0:(b + 1) * P], ps[:, 4 + j % 2, 0:(b + 1) * P], ACT.Relu).then_inc(dot_read, 1)
                    act.wait_ge(dot_read, up(dot_read))
                    if j % 4 == 3:
                        evacuate(1, 1 + j // 4)
                act.wait_ge(sdot_mm, 1)
                nc.scalar.activation(rs[:], ps[:, 2:4, 0:L], ACT.Relu).then_inc(srelu_done, 1)
                act.wait_ge(srelu_done, up(srelu_done))
                evacuate(1, 4)
                act.wait_ge(wm_mm, 1)
                nc.scalar.activation(wm[:], ps[:, 6, 64:64 + 2 * NB].rearrange("p (g b) -> p g b", g=2), ACT.Copy).then_inc(wm_ready, 1)
                act.wait_ge(wm_ready, up(wm_ready))
                evacuate(2, 0)
                evacuate(2, 1)
                take_groups([qT[:, h, :] for h in range(4)])
                act.wait_ge(ts_mm, 2)
                q_s = ps[:, 7, 0:4 * NB].rearrange("p (h b) -> p b h", b=NB)
                nc.scalar.activation(qs[0:HD, :, 0:103:34], q_s[0:HD], ACT.Copy).then_inc(act_step, 1)
                act.wait_ge(act_step, up(act_step))
                nc.scalar.activation(qs[HD:P, :, 1:104:34], q_s[HD:P], ACT.Copy).then_inc(ts_read, 1)
                act.wait_ge(ts_read, up(ts_read))
                for i in range(2, TILES):
                    evacuate(2, i)
                evacuate(3, 0)
                evacuate(3, 1)
                take_groups([kT[:, h, :] for h in range(4)])
                act.wait_ge(ts_mm, 3)
                nc.scalar.activation(kTs[:], ps[:, 7, 0:4 * NB].rearrange("p (h b) -> p h b", b=NB), ACT.Copy).then_inc(ts_read, 1)
                act.wait_ge(ts_read, up(ts_read))
                act.dma_start(k_out[bass.ds(l, 1)].rearrange("a (t p) n -> p (a t) n", p=P), zr[0][:, 0:NT, :]).then_inc(out_k, 16)
                act.dma_start(ks_out[bass.ds(l, 1)].rearrange("a p n -> (a p) n"), zr[0][0:NB, NT, :]).then_inc(out_k, 16)
                evacuate(3, 2)
                evacuate(3, 3)
                for g in range(2):
                    act.wait_ge(smx_ready, g + 1)
                    nc.scalar.activation(ps_s[:, g, :], ps[:, 2 + g, 0:L], ACT.Exp, bias=nms[:, g:g + 1],
                                         scale=ATT_SCALE, accum_out=sms[:, g:g + 1]).then_inc(sp_exp, 1)
                    act.wait_ge(sp_exp, up(sp_exp))
                evacuate(3, 4)
                act.dma_start(v_out[bass.ds(l, 1)].rearrange("a (t p) n -> p (a t) n", p=P), v_tok[:, 0:NT, :]).then_inc(out_v, 16)
                act.dma_start(vs_out[bass.ds(l, 1)].rearrange("a p n -> (a p) n"), v_tok[0:NB, NT, :]).then_inc(out_v, 16)
                act.wait_ge(vrep_mm, 1)
                for g in range(2):
                    nc.scalar.activation(vrep[:, g, :], ps[:, 6 + g, :], ACT.Copy).then_inc(vrep_ready, 1)
                    act.wait_ge(vrep_ready, up(vrep_ready))
                evacuate(4, 0)
                act.wait_ge(spt_mm, 1)
                nc.scalar.activation(pts[:], ps[:, 6, :].rearrange("p (i n) -> p i n", n=P), ACT.Copy).then_inc(spt_ready, 1)
                act.wait_ge(spt_ready, up(spt_ready))
                evacuate(4, 1)
                for n in range(ATT_FROM, 7 * TILES):
                    c, i = divmod(n, TILES)
                    for s, (slot, step) in enumerate(head_steps(c, i)):
                        attend(step)
                        if s == 0:
                            evacuate((n - 1) // TILES, (n - 1) % TILES)
                            if (c, i) == (5, 1):
                                act.wait_ge(as_mm, 1)
                                nc.scalar.activation(mix[:, 0:4, SEQ:TOK], ps[:, 7, 0:4 * NB].rearrange("p (h b) -> p h b", b=NB), ACT.Copy).then_inc(as_read, 1)
                                act.wait_ge(as_read, up(as_read))
                    if i == TILES - 1:
                        take_parts(c)
                evacuate(6, TILES - 1)
                block_out(NT - 1)
                take_groups([qT[:, h, :] for h in range(4)])
                take_parts(7)
                take_groups([kT[:, h, :] for h in range(4)])
                act.wait_ge(out_v, 32)
                evacuate(7, 0)
                zq = zr[1][0:NB, NT, :].rearrange("b (r d) -> b r d", d=32)
                zk = zr[0][0:NB, NT, :].rearrange("b (r d) -> b r d", d=32)
                vv = v_tok[0:NB, NT, :].rearrange("b (r d) -> b r d", d=HD)
                act.dma_start(qr[:], zq).then_inc(bounce, 16)
                act.dma_start(kr[:], zk).then_inc(bounce, 16)
                for j in range(2):
                    act.dma_start(vr[j:P:2, :], vv).then_inc(bounce, 16)
                evacuate(7, 1)
                evacuate(7, 2)
                gn_root(0)
                evacuate(7, 3)
                turned(0)
                gn_root(1)
                evacuate(7, 4)
                turned(1)
                act.wait_ge(sopart, 1)
                act.dma_start(op2[:].rearrange("b h j e -> b (h j) e"), op[:]).then_inc(bounce_o, 16)
                act.wait_ge(sret_ready, 1)
                act.dma_start(rets_out[bass.ds(l, 1)].rearrange("a p n -> (a p) n"), st[:]).then_inc(out_r, 16)
                gn_root(2)
                act.wait_ge(out_k, 32)
                act.wait_ge(bounce, 64)
                for n in range(KD):
                    take_item(n, wo_read)
                    square(2, 0, n, osb[:, n, HALVES[0]])
                    if n == 1:
                        turned(2)
                        gn_root(3)
                    if n == 2:
                        gn_root(4)
                        act.wait_ge(sbd_ready, NT)
                        for e in range(2):
                            act.dma_start(ret_out[bass.ds(l, 1), e::2].rearrange("a h d e -> d (a h) e"),
                                          s_bd[HD * e:HD * e + HD, :, HD * e:HD * e + HD]).then_inc(out_r, 16)
                    if n == 4:
                        turned(3)
                    if n == 5:
                        turned(4)
                act.wait_ge(gains_in, 32)
                for m in range(KD):
                    take_item(KD + m, wo_read)
                    square(2, 1, m, osb[:, m, HALVES[1]])
                    if m == 0:
                        deviation(0)
                    if 1 <= m <= 4:
                        normed(3, 0, 2 * m - 2, 2 * m - 1)
                        normed(3, 0, 2 * m - 1, 2 * m)
                    if m == 5:
                        deviation(0)
                deviation(1)
                for k in range(KD):
                    normed(3, 1, k, KD + k + 1)
                deviation(1)
                for half in range(2):
                    for i, n in enumerate(items_of(f"up{half}")):
                        kind, m, h, u = ITEMS[n]
                        act.wait_ge(up_read, 2 * FT * half + i + 1)
                        f = ff[:, m % FT, HALVES[h]]
                        nc.scalar.activation(f, f, ACT.Square).then_inc(f_ready, 1)
                        act.wait_ge(f_ready, up(f_ready))
                    if half == 0:
                        for n in items_of("down0"):
                            take_item(n, dn0_read)
                for i, n in enumerate(items_of("down1")):
                    kind, m, h, u = ITEMS[n]
                    act.wait_ge(dn1_read, i + 1)
                    square(4, h, m, osb[:, m, HALVES[h]])
                    if (m, h) == (4, 1):
                        deviation(0)
                        for k in range(4):
                            normed(5, 0, k, 2 * KD + k + 1)
                    if (m, h) == (5, 1):
                        for k in range(4, KD):
                            normed(5, 0, k, 2 * KD + k + 1)
                deviation(1)
                for k in range(KD):
                    normed(5, 1, k, 3 * KD + k + 1)
                act.wait_ge(out_ki, 32)
                act.wait_ge(out_r, 48)
                next_layer(act, l)

        @block.vector
        def _(dve):
            v = nc.vector
            v.memset(ones[:], 1.0 / D)
            v.memset(eps[:], EPS)
            for k in range(1, KD):
                dve.wait_ge(first_sq, k + 1)
                if k >= 2:
                    dve.wait_ge(first_sum, k - 1)
                v.tensor_tensor(ssum[:], ssum[:], (pt_sbw[1][:, 0:TOK], p_sbw[1])[k % 2][:], ALU.add).then_inc(first_sum, 1)
            dve.wait_ge(first_sum, KD - 1)
            v.memset(std_tok[:], 1.0)
            for q in qz:
                v.memset(q[:], 0.0)
            v.memset(s_bd[:], 0.0)
            v.memset(qis[:], 0.0)
            v.memset(qs[:], 0.0)
            v.memset(wx[:], 0.0)
            dve.drain().then_inc(zeroed, 1)
            dve.wait_ge(zeroed, 1)
            dve.wait_ge(const_in, 16 * CONSTS)
            counts, up = counter()

            def inverse(h, dst):
                dve.wait_ge(std_ready, counts.get(rstd_ready.num, 0) + 1)
                v.reciprocal(dst[:, HALVES[h]], std[:, HALVES[h]]).then_inc(rstd_ready, 1)
                dve.wait_ge(rstd_ready, up(rstd_ready))

            def rope(c, i):
                j, nh = {0: 0, 1: 1, 2: 2, 4: 3, 5: 4}[c], (NH if c else NI + 1)
                z, t, r = zr[j % 2], i, rows(i)
                dve.wait_ge(proj_read, c * TILES + t + 1)
                a = raw[(j * TILES + t) % 3][0:r, 0:nh * HD].rearrange("p (h d) -> p h d", d=HD)
                zt = z[0:r, t, 0:nh * HD]
                t2 = rope_tmp[0:r, 0:nh * HD].rearrange("p (h d) -> p h d", d=HD)
                cs = cosT[0:r, t:t + 1, :].to_broadcast([r, nh, HD])
                sn = sinT[0:r, t:t + 1, :].to_broadcast([r, nh, HD])
                v.tensor_tensor(zt.rearrange("p (h d) -> p h d", d=HD), a, cs, ALU.mult).then_inc(dve_step, 1)
                dve.wait_ge(dve_step, up(dve_step))
                v.tensor_tensor(t2[:, :, 0:32], a[:, :, 32:64], sn[:, :, 0:32], ALU.mult).then_inc(dve_step, 1)
                dve.wait_ge(dve_step, up(dve_step))
                v.tensor_tensor(t2[:, :, 32:64], a[:, :, 0:32], sn[:, :, 32:64], ALU.mult).then_inc(dve_step, 1)
                dve.wait_ge(dve_step, up(dve_step))
                v.tensor_tensor(zt, zt, rope_tmp[0:r, 0:nh * HD], ALU.add).then_inc(rope_done, 1)
                dve.wait_ge(rope_done, up(rope_done))

            def combine(j):
                b, h = 1 + j // NI, j % NI
                dve.wait_ge(dot_read, j + 1)
                r = s_sb[j % 2][:, 0:(b + 1) * P]
                if h == 0:
                    v.tensor_scalar(sc[b], r, wi[:, b, 0:1], None, ALU.mult).then_inc(comb_done, 1)
                    dve.wait_ge(comb_done, up(comb_done))
                else:
                    v.scalar_tensor_tensor(sc[b], r, wi[:, b, h:h + 1], sc[b], ALU.mult, ALU.add).then_inc(comb_done, 1)
                    dve.wait_ge(comb_done, up(comb_done))
                if h == NI - 1:
                    v.tensor_tensor(sc[b][:, b * P:(b + 1) * P], sc[b][:, b * P:(b + 1) * P], bias[:, 0:P], ALU.add).then_inc(dve_step, 1)
                    dve.wait_ge(dve_step, up(dve_step))

            def select_top(w, t8, rounds):
                for _ in range(rounds):
                    v.max(t8, w).then_inc(dve_step, 1)
                    dve.wait_ge(dve_step, up(dve_step))
                    v.match_replace(w, t8, w, MARK).then_inc(dve_step, 1)
                    dve.wait_ge(dve_step, up(dve_step))

            def block_mask(b):
                v.tensor_scalar(sc[b], sc[b], MARK, NEG, ALU.not_equal, ALU.mult).then_inc(bias_ready, 1)
                dve.wait_ge(bias_ready, up(bias_ready))

            def attend(i):
                if i < NT * NH:
                    b, c = i // NH, i % 2
                    n = (b + 1) * P
                    dve.wait_ge(att_mm, i + 1)
                    if i >= 2:
                        dve.wait_ge(p_exp, i - 1)
                    v.tensor_tensor_reduce(out=s_sb[c][:, 0:n], in0=ps[:, 4 + c, 0:n], in1=bias[:, b_at[b]:b_at[b] + n],
                                           scale=1.0, scalar=-3e38, op0=ALU.add, op1=ALU.max, accum_out=mx[:, c:c + 1]).then_inc(dve_step, 1)
                    dve.wait_ge(dve_step, up(dve_step))
                    v.tensor_scalar(neg_mx[:, c:c + 1], mx[:, c:c + 1], -ATT_SCALE, None, ALU.mult).then_inc(att_read, 1)
                    dve.wait_ge(att_read, up(att_read))
                if 1 <= i <= NT * NH:
                    j = i - 1
                    n, c = (j // NH + 1) * P, j % 2
                    dve.wait_ge(p_exp, j + 1)
                    v.reciprocal(rinv[:, c:c + 1], rsum[:, c:c + 1]).then_inc(dve_step, 1)
                    dve.wait_ge(dve_step, up(dve_step))
                    v.tensor_scalar(p_sb[c][:, 0:n], p_sb[c][:, 0:n], rinv[:, c:c + 1], None, ALU.mult).then_inc(p_ready, 1)
                    dve.wait_ge(p_ready, up(p_ready))

            def sigmoid(t, part):
                r = rows(t)
                e = raw[t % 3][0:r]
                if part == 0:
                    dve.wait_ge(gate_exp, t + 1)
                    v.tensor_scalar(e, e, 1.0, None, ALU.add).then_inc(dve_step, 1)
                    dve.wait_ge(dve_step, up(dve_step))
                if part < 2:
                    lo = e[:, part * W // 2:(part + 1) * W // 2]
                    v.reciprocal(lo, lo).then_inc(dve_step, 1)
                    dve.wait_ge(dve_step, up(dve_step))
                if part == 2:
                    dve.wait_ge(gain_ready, t + 1)
                    v.tensor_tensor(gate[0:r, t, :], gate[0:r, t, :], e, ALU.mult).then_inc(gate_ready, 1)
                    dve.wait_ge(gate_ready, up(gate_ready))

            def decayed_keys(t):
                v.tensor_tensor(kbd[:, t, :].rearrange("p (h d) -> p h d", d=HD), zr[0][:, t, :].rearrange("p (h d) -> p h d", d=HD),
                                kdec[:].rearrange("p (h o) -> p h o", o=1).to_broadcast([P, NH, HD]), ALU.mult).then_inc(kbd_ready, 1)
                dve.wait_ge(kbd_ready, up(kbd_ready))

            stv = st[:].rearrange("p (d e) -> p d e", e=HD)

            def sample_state(q):
                d8 = slice(8 * q, 8 * q + 8)
                tv = rt[0][:].rearrange("p (d e) -> p d e", e=HD)
                if q == 0:
                    dve.wait_ge(bounce, 64)
                    dve.wait_ge(state_in, 16)
                v.tensor_tensor(tv, kr[:, d8].rearrange("p (d o) -> p d o", o=1).to_broadcast([P, 8, HD]),
                                vr[:].rearrange("p (o e) -> p o e", o=1).to_broadcast([P, 8, HD]), ALU.mult).then_inc(dve_step, 1)
                dve.wait_ge(dve_step, up(dve_step))
                sq = st[:, 512 * q:512 * (q + 1)]
                done = sret_ready if q == 3 else dve_step
                v.scalar_tensor_tensor(sq, sq, gam[:], rt[0][:], ALU.mult, ALU.add).then_inc(done, 1)
                dve.wait_ge(done, up(done))
                v.tensor_tensor(tv, stv[:, d8, :], qr[:, d8].rearrange("p (d o) -> p d o", o=1).to_broadcast([P, 8, HD]), ALU.mult).then_inc(dve_step, 1)
                dve.wait_ge(dve_step, up(dve_step))
                dst = op[:] if q == 0 else rt[1][:, 0:HD]
                v.tensor_reduce(dst, rt[0][:].rearrange("p (d e) -> p e d", e=HD), AX_X, ALU.add).then_inc(dve_step, 1)
                dve.wait_ge(dve_step, up(dve_step))
                if q:
                    done = sopart if q == 3 else dve_step
                    v.tensor_tensor(op[:], op[:], rt[1][:, 0:HD], ALU.add).then_inc(done, 1)
                    dve.wait_ge(done, up(done))

            def decay_scores(c):
                for g in range(2):
                    dve.wait_ge(ra_mm, 2 * c + g + 1)
                    if c and g == 0:
                        dve.wait_ge(o_mm, c)
                    v.tensor_tensor(attm[:, 4 * g:4 * g + 4, :], ps[:, 4 + g, :].rearrange("p (h n) -> p h n", h=4),
                                    dm[:, 4 * g:4 * g + 4, :], ALU.mult).then_inc(attm_ready, 1)
                    dve.wait_ge(attm_ready, up(attm_ready))

            def next_state(c):
                dve.wait_ge(su_mm, c + 1)
                dve.wait_ge(o_mm, c + 1)
                su = ps[:, 2, :].rearrange("p (h n) -> p h n", h=4)
                for e in range(2):
                    rr, cc = slice(HD * e, HD * e + HD), slice(HD * e, HD * e + HD)
                    done = sbd_ready if e else dve_step
                    if c == 0:
                        v.tensor_copy(s_bd[rr, :, cc], su[rr, :, cc]).then_inc(done, 1)
                        dve.wait_ge(done, up(done))
                    else:
                        cd = cdec[:].rearrange("p (h o) -> p h o", o=1).to_broadcast([P, 4, HD])
                        v.tensor_tensor(s_tmp[rr], s_bd[rr, :, cc], cd[rr], ALU.mult).then_inc(dve_step, 1)
                        dve.wait_ge(dve_step, up(dve_step))
                        v.tensor_tensor(s_bd[rr, :, cc], s_tmp[rr], su[rr, :, cc], ALU.add).then_inc(done, 1)
                        dve.wait_ge(done, up(done))
                if c < NT - 1:
                    v.tensor_tensor(qTd[:], qT[:, :, (c + 1) * P:(c + 2) * P], qdec[:], ALU.mult).then_inc(qtd_ready, 1)
                    dve.wait_ge(qtd_ready, up(qtd_ready))

            oc = zr[1]

            def centre(t):
                r = rows(t)
                o = ps[:, 6 + t % 2, :] if t < NT else o_s[:]
                ov = o.rearrange("p (h d) -> p h d", d=HD)
                v.tensor_reduce(gn_mu[0:r, t, :], ov, AX_X, ALU.add).then_inc(dve_step, 1)
                dve.wait_ge(dve_step, up(dve_step))
                v.tensor_scalar(gn_mu[0:r, t, :], gn_mu[0:r, t, :], 1.0 / HD, None, ALU.mult).then_inc(dve_step, 1)
                dve.wait_ge(dve_step, up(dve_step))
                v.tensor_tensor(oc[0:r, t, :].rearrange("p (h d) -> p h d", d=HD), ov,
                                gn_mu[0:r, t, :].rearrange("p (h o) -> p h o", o=1).to_broadcast([r, NH, HD]), ALU.subtract).then_inc(o_read, 1)
                dve.wait_ge(o_read, up(o_read))

            def variance(t):
                r = rows(t)
                dve.wait_ge(osq_ready, t + 1)
                v.tensor_reduce(gn_var[0:r, t, :], osq[0:r].rearrange("p (h d) -> p h d", d=HD), AX_X, ALU.add).then_inc(gvar_ready, 1)
                dve.wait_ge(gvar_ready, up(gvar_ready))

            def finish(t):
                r = rows(t)
                dve.wait_ge(gstd_ready, t + 1)
                v.reciprocal(gn_var[0:r, t, :], gn_var[0:r, t, :]).then_inc(dve_step, 1)
                dve.wait_ge(dve_step, up(dve_step))
                ocv = oc[0:r, t, :].rearrange("p (h d) -> p h d", d=HD)
                v.tensor_tensor(ocv, ocv, gn_var[0:r, t, :].rearrange("p (h o) -> p h o", o=1).to_broadcast([r, NH, HD]), ALU.mult).then_inc(dve_step, 1)
                dve.wait_ge(dve_step, up(dve_step))
                v.tensor_tensor(oc[0:r, t, :], oc[0:r, t, :], gate[0:r, t, :], ALU.mult).then_inc(b_ready, 1)
                dve.wait_ge(b_ready, up(b_ready))

            def update(g, h, k):
                hc = HALVES[h]
                v.scalar_tensor_tensor(upd[:, hc], osb[:, k, hc], gcol[:, g, k:k + 1], rstd_post[:, hc], ALU.mult, ALU.mult).then_inc(dve_step, 1)
                dve.wait_ge(dve_step, up(dve_step))
                v.tensor_tensor(x_feat[:, k, hc], x_feat[:, k, hc], upd[:, hc], ALU.add).then_inc(x_ready, 1)
                dve.wait_ge(x_ready, up(x_ready))

            def relu(n):
                kind, m, h, u = ITEMS[n]
                dve.wait_ge(mt_done, n + 1)
                v.scalar_tensor_tensor(ff[:, m % FT, HALVES[h]], ps[:, item_bank(n), 0:span(h)], 0.0,
                                       rstd_ffn[:, HALVES[h]], ALU.max, ALU.mult).then_inc(up_read, 1)
                dve.wait_ge(up_read, up(up_read))

            def add_down(n):
                kind, m, h, u = ITEMS[n]
                dve.wait_ge(mt_done, n + 1)
                o = osb[:, m, HALVES[h]]
                v.tensor_tensor(o, o, ps[:, item_bank(n), 0:span(h)], ALU.add).then_inc(dn1_read, 1)
                dve.wait_ge(dn1_read, up(dn1_read))

            sc = {1: bias[:, 128:384], 2: bias[:, 384:768], 3: bias[:, 768:1280]}
            with dve.Fori(0, DEPTH) as l:
                counts.clear()
                dve.wait_ge(tok_std, 2)
                v.reciprocal(rtok[:, 0, :], std_tok[:]).then_inc(dve_step, 1)
                dve.wait_ge(dve_step, up(dve_step))
                v.tensor_scalar(rtok[:, 1, :], rtok[:, 0, :], HD ** -0.5, None, ALU.mult).then_inc(dve_step, 1)
                dve.wait_ge(dve_step, up(dve_step))
                v.tensor_scalar(rtok[:, 2, :], rtok[:, 0, :], NI ** -0.5 * HD ** -0.5, None, ALU.mult).then_inc(rtok_ready, 1)
                dve.wait_ge(rtok_ready, up(rtok_ready))
                for i in range(TILES):
                    rope(0, i)
                wv = wi[0:NB, NT:TILES, :]
                v.tensor_tensor(wx[:].rearrange("b g (q h) -> b (g q) h", h=32)[:, :, 0:NI],
                                exps[:].rearrange("b g (q h) -> b (g q) h", h=32)[:, :, 0:NI],
                                wv.to_broadcast([NB, NB, NI]), ALU.mult).then_inc(wx_ready, 1)
                dve.wait_ge(wx_ready, up(wx_ready))
                rope(1, 0)
                for j in range(3 * NI):
                    combine(j)
                    if j % 4 == 3:
                        rope(1, 1 + j // 4)
                rope(1, 4)
                select_top(sc[1], top8[:], 6)
                dve.wait_ge(out_ki, 32)
                dve.wait_ge(tr_mm, 3)
                dve.wait_ge(ts_mm, 1)
                rope(2, 0)
                select_top(sc[1], top8[:], TOPK_P // 8 - 6)
                block_mask(1)
                rope(2, 1)
                dve.wait_ge(ssc_mm, 1)
                v.tensor_copy(works[:], ps[0:NB, 6, P:P + L]).then_inc(ssc_read, 1)
                dve.wait_ge(ssc_read, up(ssc_read))
                select_top(works[:], tops[:], TOPK_S // 8)
                v.tensor_scalar(bias_s[:], works[:], MARK, NEG, ALU.not_equal, ALU.mult).then_inc(sbias_ready, 1)
                dve.wait_ge(sbias_ready, up(sbias_ready))
                rope(2, 2)
                select_top(sc[2], top8[:], 3)
                rope(2, 3)
                select_top(sc[2], top8[:], 3)
                rope(2, 4)
                select_top(sc[2], top8[:], TOPK_P // 8 - 6)
                block_mask(2)
                select_top(sc[3], top8[:], 8)
                for g in range(2):
                    dve.wait_ge(cache_used, 4 * g + 4)
                    v.reduce_max(mxs[:, g:g + 1], ps[:, 2 + g, 0:L], AX_X).then_inc(dve_step, 1)
                    dve.wait_ge(dve_step, up(dve_step))
                    v.tensor_scalar(nms[:, g:g + 1], mxs[:, g:g + 1], -ATT_SCALE, None, ALU.mult).then_inc(smx_ready, 1)
                    dve.wait_ge(smx_ready, up(smx_ready))
                select_top(sc[3], top8[:], 2)
                for g in range(2):
                    dve.wait_ge(sp_exp, g + 1)
                    v.reciprocal(ris[:, g:g + 1], sms[:, g:g + 1]).then_inc(dve_step, 1)
                    dve.wait_ge(dve_step, up(dve_step))
                    v.tensor_scalar(ps_s[:, g, :], ps_s[:, g, :], ris[:, g:g + 1], None, ALU.mult).then_inc(sp_ready, 1)
                    dve.wait_ge(sp_ready, up(sp_ready))
                select_top(sc[3], top8[:], TOPK_P // 8 - 10)
                block_mask(3)
                dve.wait_ge(tr_mm, 7)
                rope(4, 0)
                rope(4, 1)
                for g in range(2):
                    dve.wait_ge(cache_used, NB + 4 * g + 4)
                    dve.wait_ge(vrep_ready, g + 1)
                    v.scalar_tensor_tensor(vrep[:, g, :], vrep[:, g, :], ps_s[:, g, PAST:L], ps[:, 2 + g, :],
                                           ALU.mult, ALU.add).then_inc(dve_step, 1)
                    dve.wait_ge(dve_step, up(dve_step))
                    vg = vrep[:, g, :].rearrange("p (h d) -> p h d", d=HD)
                    v.tensor_tensor(vg, vg, dg[:].rearrange("p (h o) -> p h o", o=1).to_broadcast([P, NH, HD]), ALU.mult).then_inc(om_ready, 1)
                    dve.wait_ge(om_ready, up(om_ready))
                for n in range(ATT_FROM, 7 * TILES):
                    c, i = divmod(n, TILES)
                    if (c, i) == (5, 1):
                        dve.wait_ge(out_k, 32)
                        dve.wait_ge(tr_mm, 11)
                        dve.wait_ge(ts_mm, 3)
                    steps = head_steps(c, i)
                    for s, (slot, step) in enumerate(steps):
                        attend(step)
                        if s == 0 and n <= 6 * TILES:
                            rope((n - 1) // TILES, (n - 1) % TILES)
                        if n > 6 * TILES and s < 3:
                            sigmoid(i - 1, s)
                    if n > 6 * TILES:
                        for part in range(len(steps), 3):
                            sigmoid(i - 1, part)
                        decayed_keys(i - 1)
                sigmoid(TILES - 1, 0)
                sigmoid(TILES - 1, 1)
                sigmoid(TILES - 1, 2)
                decay_scores(0)
                sample_state(0)
                sample_state(1)
                for c in range(NT):
                    next_state(c)
                    centre(c)
                    if c < NT - 1:
                        decay_scores(c + 1)
                    variance(c)
                    if c < 2:
                        sample_state(c + 2)
                    if c == 3:
                        dve.wait_ge(bounce_o, 16)
                        v.tensor_tensor(o_s[:].rearrange("b (h e) -> b h e", e=HD), op2[:, :, 0, :], op2[:, :, 1, :], ALU.add).then_inc(dve_step, 1)
                        dve.wait_ge(dve_step, up(dve_step))
                        centre(NT)
                    finish(c)
                variance(NT)
                finish(NT)
                dve.wait_ge(gains_in, 32)
                inverse(0, rstd_post)
                for k in range(KD):
                    update(0, 0, k)
                inverse(0, rstd_ffn)
                inverse(1, rstd_post)
                ups = items_of("up0")
                for k in range(KD):
                    update(0, 1, k)
                    if k >= 4:
                        relu(ups[k - 4])
                inverse(1, rstd_ffn)
                for n in ups[4:]:
                    relu(n)
                for n in items_of("up1"):
                    relu(n)
                for n in items_of("down1"):
                    add_down(n)
                    if ITEMS[n][1:3] == (4, 1):
                        inverse(0, rstd_post)
                        for k in range(4):
                            update(2, 0, k)
                    if ITEMS[n][1:3] == (5, 1):
                        for k in range(4, KD):
                            update(2, 0, k)
                inverse(1, rstd_post)
                for k in range(KD):
                    update(2, 1, k)
                next_layer(dve, l)

        @block.gpsimd
        def _(pool):
            pool.wait_ge(zeroed, 1)
            counts, up = counter()

            def queries(b):
                blk = slice((b % 4) * P, (b % 4 + 1) * P)
                q = qz[b % 2]
                nc.gpsimd.tensor_copy(q[0:HD, 0:NH:2, :], qT[0:HD, :, blk]).then_inc(pool_step, 1)
                pool.wait_ge(pool_step, up(pool_step))
                nc.gpsimd.tensor_copy(q[HD:P, 1:NH:2, :], qT[HD:P, :, blk]).then_inc(qz_ready, 1)
                pool.wait_ge(qz_ready, up(qz_ready))

            def centred_squares(t):
                r = rows(t)
                pool.wait_ge(o_read, t + 1)
                if t:
                    pool.wait_ge(gvar_ready, t)
                nc.gpsimd.tensor_tensor(osq[0:r], zr[1][0:r, t, :], zr[1][0:r, t, :], ALU.mult).then_inc(osq_ready, 1)
                pool.wait_ge(osq_ready, up(osq_ready))

            with pool.Fori(0, DEPTH) as l:
                counts.clear()
                pool.wait_ge(tr_read, 7)
                queries(0)
                queries(1)
                pool.wait_ge(ts_read, 3)
                for b in range(NB):
                    if b >= CSLOTS:
                        pool.wait_ge(cache_used, b - CSLOTS + 1)
                    kc = cring[b % CSLOTS][:].rearrange("p (h k) -> p h k", k=L)
                    nc.gpsimd.tensor_copy(kc[:, :, PAST], kTs[:, :, b]).then_inc(knew_done, 1)
                    pool.wait_ge(knew_done, up(knew_done))
                for b in range(2, NT):
                    pool.wait_ge(att_mm, NH * (b - 1))
                    queries(b)
                pool.wait_ge(gains_in, 32)
                for t in range(TILES):
                    r = rows(t)
                    pool.wait_ge(gate_exp, t + 1)
                    nc.gpsimd.tensor_tensor(gate[0:r, t, :], gate[0:r, t, :], gret[0:r, :], ALU.mult).then_inc(gain_ready, 1)
                    pool.wait_ge(gain_ready, up(gain_ready))
                pool.wait_ge(tr_read, 15)
                pool.wait_ge(att_mm, NH * NT)
                queries(NT)
                queries(NT + 1)
                for c in range(NT):
                    centred_squares(c)
                    if c < 2:
                        pool.wait_ge(ra_mm, 2 * (c + 1))
                        queries(NT + 2 + c)
                centred_squares(NT)
                for norm, h, k in SQUARES:
                    pool.wait_ge(sq_ready, square_number(norm, h, k)[0])
                    if k:
                        hc = HALVES[h]
                        added = square_number(norm, h, k)[1]
                        nc.gpsimd.tensor_tensor(ssum[:, hc], ssum[:, hc], sqr[added % 2][:, 0:span(h)], ALU.add).then_inc(sq_used, 1)
                        pool.wait_ge(sq_used, up(sq_used))
                next_layer(pool, l)

def constants():
    f = np.float32
    half = HD // 2
    inv = (f(10000.0) ** (-np.arange(half, dtype=f) / f(half))).astype(f)
    pos = np.zeros((P, TILES), f)
    pos[:, 0:NT] = np.arange(SEQ, dtype=f).reshape(NT, P).T
    pos[:, NT] = PAST
    ang = (pos[:, :, None] * inv[None, None, :]).astype(f)
    c, s = np.cos(ang).astype(f), np.sin(ang).astype(f)
    lg = np.log1p(-np.exp2(-5.0 - np.arange(NH)))
    i = np.arange(P)
    diff = i[None, :] - i[:, None]
    dmask = np.where(diff[:, None, :] >= 0, np.exp(np.maximum(diff, 0)[:, None, :] * lg[None, :, None]), 0.0)
    pair = np.arange(P)[:, None] // HD + 2 * np.arange(4)[None, :]
    qdec = np.exp((i[None, None, :] + 1.0) * lg[pair][:, :, None])
    expand = np.zeros((NB, 2, P), f)
    for b in range(NB):
        expand[b, b // 4, 32 * (b % 4):32 * (b % 4) + 32] = 1.0
    diag = np.zeros((P, NH), f)
    for r in range(P):
        if r % 32 < NH:
            diag[r, r % 32] = 1.0
    sum_parts = np.zeros((P, NB), f)
    for q4 in range(32 - NB, P, 32):
        sum_parts[q4:q4 + NB] = np.eye(NB)
    return dict(
        sum_parts=sum_parts, tab_cos=np.concatenate([c, c], -1), tab_sin=np.concatenate([-s, s], -1), dmask=dmask.astype(f),
        k_decay=np.exp((P - 1.0 - i)[:, None] * lg[None, :]).astype(f), q_decay=qdec.astype(f),
        c_decay=np.exp(P * lg[pair]).astype(f),
        s_gamma=np.exp(lg[(np.arange(P) // 2) % NH]).astype(f)[:, None], ident=np.eye(P, dtype=f),
        expand=expand, select=np.ascontiguousarray(expand.transpose(2, 1, 0)), diag=diag,
        causal=np.where(i[None, :] <= i[:, None], 0.0, NEG).astype(f))


def kernel(x_prompt, x_sample, cache_k, cache_v, cache_kidx, state_ret, page_table, w_in, w_out, g_ret,
           g_mix_pre, g_mix_post, g_ffn_pre, g_ffn_post, w_up, w_down):
    import concourse.bacc as bacc
    from concourse.bass_utils import run_bass_kernel_spmd

    A = lambda a: np.asarray(a)
    x = np.concatenate([A(x_prompt).reshape(SEQ, D), A(x_sample).reshape(NB, D)])
    n_pool = cache_k.shape[1]
    w_in = A(w_in)
    a3, idx = 3 * W, W_IDX
    starts = [0, W, 2 * W, a3 + idx, a3 + idx + W, a3 + idx + 3 * W, a3 + idx + 2 * W]

    def moving(w):
        n = w.shape[-1]
        return w.reshape(-1, 2, 4, P, n).transpose(0, 1, 3, 2, 4).reshape(-1, 2, P, 4 * n)

    def stationary(w, kn, per):
        m = w.shape[-1] // P
        v = w.reshape(DEPTH, kn, P, m, P).transpose(0, 3, 2, 1, 4).reshape(DEPTH, m // per, per, P, kn * P)
        return v.transpose(0, 1, 3, 2, 4).reshape(DEPTH, m // per, P, per * kn * P)

    w_up, w_down = A(w_up), A(w_down)
    parts = [moving(w_in[:, :, c:c + W]) for c in starts] + [stationary(A(w_out), KD, 2)]
    for half in range(2):
        f0, f1 = half * FF // 2, (half + 1) * FF // 2
        parts += [stationary(w_up[:, :, f0:f1], KD, 2), stationary(w_down[:, f0:f1, :], FT, 1)]
    arrays = dict(
        x=x.T.reshape(KD, P, TOK).transpose(1, 0, 2),
        w_idx=moving(w_in[list(range(DEPTH)) + [0], :, a3:a3 + idx]),
        w_all=np.concatenate(parts, 1),
        gains=np.stack([A(g).reshape(DEPTH, KD, P).transpose(0, 2, 1) for g in
                        (g_mix_post, g_ffn_pre, g_ffn_post, np.roll(A(g_mix_pre), -1, 0))], 2),
        g_first=A(g_mix_pre)[0].reshape(KD, P).T,
        g_ret=A(g_ret),
        cache_k=A(cache_k).reshape(DEPTH, n_pool, PAGE, W).transpose(0, 1, 3, 2),
        cache_v=A(cache_v).reshape(DEPTH, n_pool, PAGE, W),
        cache_ki=A(cache_kidx).transpose(0, 1, 3, 2),
        state=A(state_ret).reshape(DEPTH, P, 2048),
        pages=A(page_table).astype(np.int32).reshape(1, NB * NPAGES), **constants())
    outs = dict(y=(P, KD, TOK), k_out=(DEPTH, SEQ, W), v_out=(DEPTH, SEQ, W), ki_out=(DEPTH, SEQ, HD),
                ret_out=(DEPTH, NH, HD, HD), ks_out=(DEPTH, NB, W), vs_out=(DEPTH, NB, W),
                kis_out=(DEPTH, NB, HD), rets_out=(DEPTH, P, 2048))
    nc = bacc.Bacc("TRN2", target_bir_lowering=False, num_devices=1, dynamic_dma_scratch_size=1024)
    args, given = {}, {}
    for name, a in arrays.items():
        a = np.ascontiguousarray(a)
        given[f"in_{name}"] = a
        args[name] = nc.dram_tensor(f"in_{name}", a.shape, mybir.dt.from_np(a.dtype), kind="ExternalInput").ap()
    for name, shape in outs.items():
        args[name] = nc.dram_tensor(f"o_{name}", shape, F32, kind="ExternalOutput").ap()
    build(nc, **args)
    r = run_bass_kernel_spmd(nc, [given], core_ids=[0]).results[0]
    o = {name: r[f"o_{name}"] for name in outs}
    yy = np.asarray(o["y"]).transpose(2, 1, 0).reshape(TOK, D)
    return (yy[0:SEQ].reshape(1, SEQ, D), yy[SEQ:].reshape(NB, 1, D),
            o["k_out"].reshape(DEPTH, 1, SEQ, NH, HD), o["v_out"].reshape(DEPTH, 1, SEQ, NH, HD),
            o["ki_out"].reshape(DEPTH, 1, SEQ, HD), o["ret_out"].reshape(DEPTH, 1, NH, HD, HD),
            o["ks_out"].reshape(DEPTH, NB, 1, NH, HD), o["vs_out"].reshape(DEPTH, NB, 1, NH, HD),
            o["kis_out"].reshape(DEPTH, NB, 1, HD), o["rets_out"].reshape(DEPTH, NB, NH, HD, HD))
```
